# Optimizing a Trainium2 kernel written in Bass

```python
import jax, jax.numpy as jnp
from jax import lax
import numpy as np

D_MODEL = 1024
BATCH = 1
SEQ = 1024
DEPTH = 1
DEC_BATCH = 8
DEC_SEQ = 8
PAST_LEN = 4096
PAGE_SIZE = 128

ATT_WIDTH = D_MODEL // 2
CONV_CH = D_MODEL - ATT_WIDTH
HEAD_DIM = 64
N_ATT_HEADS = ATT_WIDTH // HEAD_DIM
DILATED_BRANCHES = ((128, 1), (512, 4), (2048, 16))
W_MAX = 2048
Q_BLOCK = 128
CONV_K = 31
IN_COLS = 3 * ATT_WIDTH + 2 * CONV_CH
N_KEYS = 128
N_EXPERTS = N_KEYS * N_KEYS
PEER_HEADS = 8
PEER_KEY_DIM = 256
PEER_TOPK = 16
PEER_BLOCK = 256
ALPHA = (2.0 * DEPTH) ** 0.25
BETA = (8.0 * DEPTH) ** -0.25
LN_EPS = 1e-5

kernel_name = "hymba_conformer_dilated_peer_step"

def _layer_norm(x, g, b):
    xf = x.astype(jnp.float32)
    mu = jnp.mean(xf, -1, keepdims=True)
    var = jnp.mean(jnp.square(xf - mu), -1, keepdims=True)
    return ((xf - mu) * lax.rsqrt(var + LN_EPS) * g.astype(jnp.float32) + b.astype(jnp.float32)).astype(x.dtype)

def _masked_softmax_stats(s, mask):
    s = jnp.where(mask, s, -jnp.inf)
    m = jnp.max(s, -1, keepdims=True)
    p = jnp.exp(s - m)
    den = jnp.sum(p, -1, keepdims=True)
    return p / den, m[..., 0] + jnp.log(den[..., 0])

def _combine_branches(outs, lses, dtype):
    wts = jax.nn.softmax(jnp.stack(lses, 0), axis=0)
    o = outs[0] * wts[0][..., None]
    for i in range(1, len(outs)):
        o = o + outs[i] * wts[i][..., None]
    return o.astype(dtype)

def _in_proj(x, w_in):
    B, T, _ = x.shape
    z = jnp.einsum('btd,df->btf', x, w_in)
    q = z[..., 0:ATT_WIDTH].reshape(B, T, N_ATT_HEADS, HEAD_DIM)
    k = z[..., ATT_WIDTH:2 * ATT_WIDTH].reshape(B, T, N_ATT_HEADS, HEAD_DIM)
    v = z[..., 2 * ATT_WIDTH:3 * ATT_WIDTH].reshape(B, T, N_ATT_HEADS, HEAD_DIM)
    a = z[..., 3 * ATT_WIDTH:3 * ATT_WIDTH + CONV_CH]
    g = z[..., 3 * ATT_WIDTH + CONV_CH:]
    glu = a * jax.nn.sigmoid(g)
    return q, k, v, glu

def _dilated_attn_prompt(q, k, v):
    B, S, H, E = q.shape
    scale = HEAD_DIM ** -0.5
    pad = ((0, 0), (W_MAX, 0), (0, 0), (0, 0))
    kp = jnp.pad(k, pad)
    vp = jnp.pad(v, pad)

    def block(t0):
        qb = lax.dynamic_slice_in_dim(q, t0, Q_BLOCK, axis=1)
        outs, lses = [], []
        for w, d in DILATED_BRANCHES:
            L = w + Q_BLOCK
            kb = lax.dynamic_slice_in_dim(kp, t0 + W_MAX - w, L, axis=1)
            vb = lax.dynamic_slice_in_dim(vp, t0 + W_MAX - w, L, axis=1)
            qr = qb.reshape(B, Q_BLOCK // d, d, H, E)
            kr = kb.reshape(B, L // d, d, H, E)
            vr = vb.reshape(B, L // d, d, H, E).astype(jnp.float32)
            s = jnp.einsum('birhe,bjrhe->brhij', qr, kr,
                           preferred_element_type=jnp.float32) * scale
            i = jnp.arange(Q_BLOCK // d)[:, None]
            j = jnp.arange(L // d)[None, :]
            r = jnp.arange(d)[:, None, None]
            rel = j - i
            key_pos = t0 - w + j * d + r
            mask = (rel >= 0) & (rel <= w // d) & (key_pos >= 0)
            p, lse = _masked_softmax_stats(s, mask[:, None])
            o = jnp.einsum('brhij,bjrhe->birhe', p, vr)
            outs.append(o.reshape(B, Q_BLOCK, H, E))
            lses.append(lse.transpose(0, 3, 1, 2).reshape(B, Q_BLOCK, H))
        return _combine_branches(outs, lses, q.dtype)

    ob = lax.map(block, jnp.arange(S // Q_BLOCK) * Q_BLOCK)
    return ob.transpose(1, 0, 2, 3, 4).reshape(B, S, H, E)

def _dilated_attn_sample(q, k_all, v_all):
    B, T, H, E = q.shape
    Lb = k_all.shape[1] - T
    scale = HEAD_DIM ** -0.5
    outs, lses = [], []
    for w, d in DILATED_BRANCHES:
        n = w // d + 1
        idx = Lb + jnp.arange(T)[:, None] - d * jnp.arange(n)[None, :]
        valid = idx >= 0
        idxc = jnp.maximum(idx, 0)
        kg = jnp.take(k_all, idxc, axis=1)
        vg = jnp.take(v_all, idxc, axis=1).astype(jnp.float32)
        s = jnp.einsum('bthe,btnhe->bhtn', q, kg,
                       preferred_element_type=jnp.float32) * scale
        p, lse = _masked_softmax_stats(s, valid)
        outs.append(jnp.einsum('bhtn,btnhe->bthe', p, vg))
        lses.append(lse.transpose(0, 2, 1))
    return _combine_branches(outs, lses, q.dtype)

def _conv_module(glu, conv_past, conv_w, conv_b, ln_g, ln_b):
    xpad = jnp.concatenate([conv_past, glu], axis=1)
    y = lax.conv_general_dilated(xpad, conv_w[:, None, :].astype(xpad.dtype), window_strides=(1,),
                                 padding='VALID', dimension_numbers=('NWC', 'WIO', 'NWC'),
                                 feature_group_count=CONV_CH)
    y = _layer_norm(y + conv_b, ln_g, ln_b)
    return jax.nn.silu(y)

def _peer(x, w_query, sub_keys, expert_u, expert_v):
    B, T, D = x.shape
    xt = x.reshape(B * T, D)
    n = xt.shape[0]
    n_pad = (-n) % PEER_BLOCK
    blocks = jnp.pad(xt, ((0, n_pad), (0, 0))).reshape(-1, PEER_BLOCK, D)
    half = PEER_KEY_DIM // 2

    def block(xb):
        q = (xb @ w_query).reshape(PEER_BLOCK, PEER_HEADS, 2, half)
        s = jnp.einsum('thpc,hpkc->thpk', q, sub_keys, preferred_element_type=jnp.float32)
        top_s, top_i = lax.top_k(s, PEER_TOPK)
        cand_s = (top_s[:, :, 0, :, None] + top_s[:, :, 1, None, :]).reshape(PEER_BLOCK, PEER_HEADS, -1)
        cand_e = (top_i[:, :, 0, :, None] * N_KEYS + top_i[:, :, 1, None, :]).reshape(PEER_BLOCK, PEER_HEADS, -1)
        best_s, best_j = lax.top_k(cand_s, PEER_TOPK)
        experts = jnp.take_along_axis(cand_e, best_j, axis=-1)
        gate = jax.nn.softmax(best_s, axis=-1).reshape(PEER_BLOCK, -1)
        e_flat = experts.reshape(PEER_BLOCK, -1)
        u = jnp.take(expert_u, e_flat, axis=0)
        vv = jnp.take(expert_v, e_flat, axis=0)
        act = jax.nn.gelu(jnp.einsum('td,tkd->tk', xb, u, preferred_element_type=jnp.float32),
                          approximate=False)
        coef = (gate * act).astype(vv.dtype)
        return jnp.einsum('tk,tkd->td', coef, vv)

    out = lax.map(block, blocks).reshape(-1, D)[:n]
    return out.reshape(B, T, D).astype(x.dtype)

def _finish(x, att, conv, w_out, ln1_g, ln1_b, w_query, sub_keys, expert_u, expert_v, ln2_g, ln2_b):
    B, T, _ = x.shape
    mixed = jnp.concatenate([att.reshape(B, T, ATT_WIDTH), conv], axis=-1)
    mix = jnp.einsum('btf,fd->btd', mixed, w_out)
    x1 = _layer_norm(ALPHA * x + mix, ln1_g, ln1_b)
    return _layer_norm(ALPHA * x1 + _peer(x1, w_query, sub_keys, expert_u, expert_v), ln2_g, ln2_b)

def setup_inputs(seed: int = 0) -> dict:
    key = jax.random.key(seed)
    ks = jax.random.split(key, 20)
    f32 = jnp.float32
    wb = min(W_MAX, PAST_LEN)
    col_scale = jnp.concatenate([jnp.ones((2 * ATT_WIDTH,), f32),
                                 jnp.full((ATT_WIDTH + 2 * CONV_CH,), BETA, f32)])
    return {
        "x_prompt": jax.random.normal(ks[0], (BATCH, SEQ, D_MODEL), f32),
        "x_sample": jax.random.normal(ks[1], (DEC_BATCH, DEC_SEQ, D_MODEL), f32),
        "cache_k_win": jax.random.normal(ks[2], (DEPTH, DEC_BATCH, wb, N_ATT_HEADS, HEAD_DIM), f32),
        "cache_v_win": BETA * jax.random.normal(ks[3], (DEPTH, DEC_BATCH, wb, N_ATT_HEADS, HEAD_DIM), f32),
        "state_conv": 0.5 * jax.random.normal(ks[4], (DEPTH, DEC_BATCH, CONV_K - 1, CONV_CH), f32),
        "w_in": jax.random.normal(ks[5], (DEPTH, D_MODEL, IN_COLS), f32) * D_MODEL ** -0.5 * col_scale,
        "w_out": jax.random.normal(ks[6], (DEPTH, D_MODEL, D_MODEL), f32) * D_MODEL ** -0.5 * BETA,
        "conv_w": jax.random.normal(ks[7], (DEPTH, CONV_K, CONV_CH), f32) * CONV_K ** -0.5,
        "conv_b": 0.02 * jax.random.normal(ks[8], (DEPTH, CONV_CH), f32),
        "conv_ln_g": 1.0 + 0.02 * jax.random.normal(ks[9], (DEPTH, CONV_CH), f32),
        "conv_ln_b": 0.02 * jax.random.normal(ks[10], (DEPTH, CONV_CH), f32),
        "ln1_g": 1.0 + 0.02 * jax.random.normal(ks[11], (DEPTH, D_MODEL), f32),
        "ln1_b": 0.02 * jax.random.normal(ks[12], (DEPTH, D_MODEL), f32),
        "w_query": jax.random.normal(ks[13], (DEPTH, D_MODEL, PEER_HEADS * PEER_KEY_DIM), f32) * D_MODEL ** -0.5,
        "sub_keys": jax.random.normal(ks[14], (DEPTH, PEER_HEADS, 2, N_KEYS, PEER_KEY_DIM // 2), f32) * (PEER_KEY_DIM // 2) ** -0.5,
        "expert_u": jax.random.normal(ks[15], (DEPTH, N_EXPERTS, D_MODEL), f32) * D_MODEL ** -0.5 * BETA,
        "expert_v": jax.random.normal(ks[16], (DEPTH, N_EXPERTS, D_MODEL), f32) * 0.5 * BETA,
        "ln2_g": 1.0 + 0.02 * jax.random.normal(ks[17], (DEPTH, D_MODEL), f32),
        "ln2_b": 0.02 * jax.random.normal(ks[18], (DEPTH, D_MODEL), f32),
    }

def reference(x_prompt, x_sample, cache_k_win, cache_v_win, state_conv,
              w_in, w_out, conv_w, conv_b, conv_ln_g, conv_ln_b,
              ln1_g, ln1_b, w_query, sub_keys, expert_u, expert_v, ln2_g, ln2_b):
    hp, hs = x_prompt, x_sample
    kp_rows, vp_rows, cp_rows, ks_rows, vs_rows, cs_rows = [], [], [], [], [], []
    for l in range(DEPTH):
        S = hp.shape[1]
        q, k, v, glu = _in_proj(hp, w_in[l])
        att = _dilated_attn_prompt(q, k, v)
        conv = _conv_module(glu, jnp.zeros((hp.shape[0], CONV_K - 1, CONV_CH), glu.dtype),
                            conv_w[l], conv_b[l], conv_ln_g[l], conv_ln_b[l])
        keep_p = min(W_MAX, S)
        kp_rows.append(k[:, S - keep_p:])
        vp_rows.append(v[:, S - keep_p:])
        cp_rows.append(glu[:, S - (CONV_K - 1):])
        hp = _finish(hp, att, conv, w_out[l], ln1_g[l], ln1_b[l], w_query[l], sub_keys[l],
                     expert_u[l], expert_v[l], ln2_g[l], ln2_b[l])

        T = hs.shape[1]
        q2, k2, v2, glu2 = _in_proj(hs, w_in[l])
        k_all = jnp.concatenate([cache_k_win[l].astype(k2.dtype), k2], axis=1)
        v_all = jnp.concatenate([cache_v_win[l].astype(v2.dtype), v2], axis=1)
        att2 = _dilated_attn_sample(q2, k_all, v_all)
        conv_in = jnp.concatenate([state_conv[l].astype(glu2.dtype), glu2], axis=1)
        conv2 = _conv_module(glu2, state_conv[l].astype(glu2.dtype),
                             conv_w[l], conv_b[l], conv_ln_g[l], conv_ln_b[l])
        L_all = k_all.shape[1]
        keep_s = min(W_MAX, L_all)
        ks_rows.append(k_all[:, L_all - keep_s:])
        vs_rows.append(v_all[:, L_all - keep_s:])
        cs_rows.append(conv_in[:, conv_in.shape[1] - (CONV_K - 1):])
        hs = _finish(hs, att2, conv2, w_out[l], ln1_g[l], ln1_b[l], w_query[l], sub_keys[l],
                     expert_u[l], expert_v[l], ln2_g[l], ln2_b[l])

    new_k_prompt = jnp.stack(kp_rows, 0)
    new_v_prompt = jnp.stack(vp_rows, 0)
    new_conv_prompt = jnp.stack(cp_rows, 0)
    new_k_sample = jnp.stack(ks_rows, 0)
    new_v_sample = jnp.stack(vs_rows, 0)
    new_conv_sample = jnp.stack(cs_rows, 0)
    return (hp, hs, new_k_prompt, new_v_prompt, new_conv_prompt, new_k_sample, new_v_sample, new_conv_sample)


_drawn_inputs = setup_inputs


def setup_inputs(seed=0):
    import zlib

    import numpy as np

    out = dict(_drawn_inputs(seed))
    spreads = {}
    factors = {'conv_b': 3.462,
     'conv_ln_g': 21.811,
     'conv_ln_b': 45.209,
     'ln2_g': 23.662,
     'ln2_b': 23.822}
    for name, (base, spread) in spreads.items():
        noise = np.random.default_rng([zlib.crc32(name.encode()), seed]).standard_normal(out[name].shape)
        drawn = base * np.exp(spread * noise) if base else spread * noise
        out[name] = __import__('jax').numpy.asarray(drawn.astype(out[name].dtype))
    for name, factor in factors.items():
        out[name] = (out[name] * factor).astype(out[name].dtype)
    return out
```

```python
from contextlib import ExitStack

import numpy as np

import concourse.bass as bass
import concourse.mybir as mybir

F32 = mybir.dt.float32
U32 = mybir.dt.uint32
ALU = mybir.AluOpType
ACT = mybir.ActivationFunctionType
AX = mybir.AxisListType

P = 128
D = 1024
KD = D // P
SEQ = 1024
NB, NT = 8, 8
NS = NB * NT
TOK = SEQ + NS
PT = SEQ // P
TILES = PT + 1
H, E = 8, 64
AW = H * E
CC = D - AW
CT = CC // P
CK = 31
PAST = CK - 1
WIN = 2048
SCALE = E ** -0.5
BRANCHES = ((128, 1), (512, 4), (2048, 16))
MASKED = -1e30
LOWEST = -3.0e38
ALPHA = 2.0 ** 0.25
EPS = 1e-5
PH = 8
NK = 128
TOP = 16
SLOTS = PH * TOP
KEYC = 128

FAR = WIN - 512
NFAR = FAR // 16
FSL = NT
LSL = 4
KEYS = NT + FSL * NFAR + LSL * P
HALF = FSL // 2 * NFAR
C_NEW, C_FAR2, C_NEAR = HALF, HALF + NT, 2 * HALF + NT

ROWS_OUT = TILES + 2
SB = (4, 5, 6)
O_PV = 384
W_RING = 4
U_RING = 8
V_RING = 8
DG_RING = 4


def _count(d):
    return sum((d >= 0) & (d <= w) & (d % s == 0) for w, s in BRANCHES)


def _bias(d):
    n = _count(d)
    return np.where(n > 0, np.log(np.maximum(n, 1)) / SCALE, MASKED).astype(np.float32)


def shape_constants():
    q = np.arange(P)[:, None]
    prompt = _bias(q + (SEQ - P) - np.arange(SEQ)[None, :])
    pos = np.empty(KEYS, np.int64)
    far = np.arange(NFAR)
    for r in range(FSL):
        at = r * NFAR if r < 4 else C_FAR2 + (r - 4) * NFAR
        pos[at:at + NFAR] = 16 * far + r
    pos[C_NEW:C_NEW + NT] = WIN + np.arange(NT)
    for s in range(LSL):
        pos[C_NEAR + s * P:C_NEAR + (s + 1) * P] = FAR + LSL * np.arange(P) + s
    t = np.tile(np.arange(NT), H)[:, None]
    sample = _bias(WIN + t - pos[None, :])
    return {
        "c_ident": np.eye(P, dtype=np.float32),
        "c_prompt_bias": prompt,
        "c_sample_bias": sample,
        "c_iota": np.tile(np.arange(TOP, dtype=np.float32), (P, 1)),
    }


def build(nc, I, O):
    y_p, y_s, nk_p, nv_p, nc_p, nk_s, nv_s, nc_s = O
    x1_d = nc.dram_tensor("x1_scratch", (TILES * P, D), F32, kind="Internal").ap()

    ctx = ExitStack()
    with ctx:
        base = nc.sbuf_base
        base = (base + 63) // 64 * 64
        names = [0]

        def at(off, shape, dt=F32):
            names[0] += 1
            return nc.alloc_sbuf_tensor_at(f"t{names[0]}", shape, dt, offset=base + off)

        def sem(name):
            return ctx.enter_context(nc.semaphore(name))

        psum = ctx.enter_context(nc.psum_tensor("psum", [P, 8 * 512], F32))
        bank = [psum[:, i * 512:(i + 1) * 512] for i in range(8)]

        o_a = 0
        o_b = o_a + KD * TOK * 4
        o_c = o_b + KD * D * 4
        o_d = o_c + 2 * CT * SEQ * 4 + PT * AW * 4
        o_f = o_d + CT * (PAST + SEQ) * 4 + CT * NB * (PAST + NT) * 4
        o_g = o_f + CT * TOK * 4
        xT = at(o_a, [P, KD, TOK])
        mixedT = at(o_a, [P, KD, TOK])
        w_v = at(o_b, [P, KD, AW])
        w_ring = at(o_b + KD * AW * 4, [P, W_RING, KD, P])
        w_out = at(o_b, [P, KD, D])
        qT = at(o_c, [P, CT, SEQ])
        kT = at(o_c + CT * SEQ * 4, [P, CT, SEQ])
        v = at(o_c + 2 * CT * SEQ * 4, [P, PT, AW])
        k_cache = [at(o, [P, FSL + LSL, AW]) for o in (o_c, o_b)]
        v_cache = at(o_c + (FSL + LSL) * AW * 4, [P, FSL + LSL, AW])
        gluP = at(o_d, [P, CT, PAST + SEQ])
        gluS = at(o_d + CT * (PAST + SEQ) * 4, [P, CT, NB, PAST + NT])
        conv = at(o_f, [P, CT, TOK])
        sm = at(o_g, [P, 2, SEQ])
        pT = at(o_g + 8192, [P, 2, SEQ])
        att = at(o_g + 16384, [P, 2, AW])
        o_h = o_g + 20480
        kTc = at(o_g, [P, CT, FSL * NFAR + LSL * P])
        xt = at(o_h, [P, 2, D])
        o_i = o_h + 8192
        bias_p = at(o_i, [P, SEQ])
        sig = at(o_i + 4096, [P, 2, 512])
        sms = at(o_i, [NS, KEYS])
        o_j = o_i + max(8192, KEYS * 4)
        bias_s = at(o_j, [NS, KEYS])
        o_k = o_j + KEYS * 4
        ident = at(o_k, [P, P])
        qTs = at(o_k + 512, [P, CT, NS])
        kTs = at(o_k + 1536, [P, CT, NS])
        glu_new = at(o_k + 2560, [P, CT, NS])
        cwT = at(o_k + 3584, [P, CT, CK + 3])
        o_l = o_k + 3584 + 576
        pTs = at(o_l, [P, FSL + LSL + 1, NS])
        small = at(o_l + 3328, [P, 64])
        o_m = o_l + 3328 + 256
        kst = at(o_m, [P, 2, AW])
        v_new = at(o_d, [NT, NB, AW])
        qbd = at(o_g + CT * 1280 * 4, [P, CT, NB, NS])
        assert CT * 1280 * 4 == 20480
        cw = at(o_f, [CK + 3, CC])
        st_in = at(o_f + 2048, [120, 2, CC])
        vs = at(o_f + 8192, [NS, AW])
        end_front = o_m + 4096
        assert base + end_front <= nc.sbuf_usable_end, (base + end_front, nc.sbuf_usable_end)
        lnw = at(o_g, [P, 2, D])
        xr = at(o_g + 8192, [P, 2, D])
        res = at(o_g + 16384, [P, 2, D])
        x1o = at(o_g + 24576, [P, 2, D])
        assert o_g + 32768 <= o_j
        stat = at(o_l, [P, 2, 32])
        cn = at(o_m, [P, 2, CC])
        cstat = at(o_l + 256, [P, 2, 16])

        u_buf = at(0, [P, U_RING, D])
        v_buf = at(U_RING * D * 4, [P, V_RING, D])
        sk_in = at(U_RING * D * 4, [P, PH * 2, KEYC])
        assert (U_RING + V_RING) * D * 4 <= o_c
        wq = at(o_c, [P, KD, PH * 2 * KEYC])
        p0 = o_c + KD * PH * 2 * KEYC * 4
        assert p0 <= o_f
        skT = at(p0, [P, PH * 2, NK]); p0 += PH * 2 * NK * 4
        x1n = at(p0, [P, D]); p0 += D * 4
        x1c = at(p0, [P, D]); p0 += D * 4
        x1T = at(p0, [P, KD, P]); p0 += KD * P * 4
        junk = at(p0, [P, 2, D]); p0 += 2 * D * 4
        lnw2 = at(p0, [P, 2, D]); p0 += 2 * D * 4
        yt = at(p0, [P, D]); p0 += D * 4
        diag = at(p0, [P, DG_RING, P]); p0 += DG_RING * P * 4
        qh = at(p0, [P, 2, 2 * P]); p0 += 4 * P * 4
        sh = at(p0, [P, 2, 2 * NK]); p0 += 4 * NK * 4
        s2 = at(p0, [P, 2, NK]); p0 += 2 * NK * 4
        cand = at(p0, [P, TOP * TOP]); p0 += TOP * TOP * 4
        cand2 = at(p0, [P, TOP * TOP]); p0 += TOP * TOP * 4
        eq = at(p0, [P, 2, TOP * TOP]); p0 += 2 * TOP * TOP * 4
        iden2 = at(p0, [P, P]); p0 += P * 4
        iota = at(p0, [P, TOP]); p0 += TOP * 4
        tv = at(p0, [P, 2, TOP]); p0 += 2 * TOP * 4
        ti = at(p0, [P, 2, TOP], U32); p0 += 2 * TOP * 4
        tif = at(p0, [P, 2, TOP]); p0 += 2 * TOP * 4
        bv = at(p0, [P, TOP]); p0 += TOP * 4
        bj = at(p0, [P, TOP], U32); p0 += TOP * 4
        ab = at(p0, [P, 2, TOP], U32); p0 += 2 * TOP * 4
        abf = at(p0, [P, 2, TOP]); p0 += 2 * TOP * 4
        eif = at(p0, [P, 2, TOP]); p0 += 2 * TOP * 4
        ex = at(p0, [P, 2, TOP]); p0 += 2 * TOP * 4
        den = at(p0, [P, 4]); p0 += 32
        rdn = at(p0, [P, 4]); p0 += 32
        idn = at(p0, [P, SLOTS], U32); p0 += SLOTS * 4
        idc = at(p0, [P, SLOTS], U32); p0 += SLOTS * 4
        gtn = at(p0, [P, SLOTS]); p0 += SLOTS * 4
        gtc = at(p0, [P, SLOTS]); p0 += SLOTS * 4
        dots = at(p0, [P, SLOTS]); p0 += SLOTS * 4
        gel = at(p0, [P, SLOTS]); p0 += SLOTS * 4
        coef = at(p0, [P, SLOTS]); p0 += SLOTS * 4
        st2 = at(p0, [P, 32]); p0 += 128
        assert base + p0 <= nc.sbuf_usable_end, (base + p0, nc.sbuf_usable_end)

        const_in = sem("const_in")
        aux_in = sem("aux_in")
        x_in = [sem(f"x_in{i}") for i in range(2)]
        x_used = sem("x_used")
        xT_ready = sem("xT_ready")
        aux_tr = sem("aux_tr")
        aux_ready = sem("aux_ready")
        w_in_s = [sem(f"w_in{i}") for i in range(W_RING)]
        wv_in = sem("wv_in")
        proj_done = sem("proj_done")
        proj_evac = sem("proj_evac")
        glu_done = sem("glu_done")
        v_done = sem("v_done")
        v_evac = sem("v_evac")
        row_tr = sem("row_tr")
        row_evac = sem("row_evac")
        row_out = [sem(f"row_out{i}") for i in range(2)]
        out_dma = sem("out_dma")
        v_out = sem("v_out")
        vn_out = sem("vn_out")
        vn_in = sem("vn_in")
        pads = sem("pads")
        glu_s = sem("glu_s")
        dv = sem("dv")
        cv = sem("cv")
        s_done = sem("s_done")
        sm_done = sem("sm_done")
        nm_done = sem("nm_done")
        exp_done = sem("exp_done")
        p_tr = sem("p_tr")
        pT_ready = sem("pT_ready")
        pv_done = sem("pv_done")
        att_done = sem("att_done")
        att_tr = sem("att_tr")
        att_T = sem("att_T")
        kc_in = [sem(f"kc_in{i}") for i in range(2)]
        vc_in = sem("vc_in")
        qbd_done = sem("qbd_done")
        kc_tr = sem("kc_tr")
        kc_evac = sem("kc_evac")
        ss_done = sem("ss_done")
        ssm_done = sem("ssm_done")
        snm_done = sem("snm_done")
        sexp_done = sem("sexp_done")
        sp_done = sem("sp_done")
        sp_tr = sem("sp_tr")
        spT_ready = sem("spT_ready")
        spv_done = sem("spv_done")
        satt_T = sem("satt_T")
        c_tr = sem("c_tr")
        c_var = sem("c_var")
        c_std = sem("c_std")
        c_norm = sem("c_norm")
        c_tr2 = sem("c_tr2")
        c_T = sem("c_T")
        wout_in = sem("wout_in")
        lnw_in = sem("lnw_in")
        xr_in = [sem(f"xr_in{i}") for i in range(2)]
        mix_done = sem("mix_done")
        res_done = sem("res_done")
        l_var = sem("l_var")
        l_std = sem("l_std")
        x1_done = sem("x1_done")
        x1_out = [sem(f"x1_out{i}") for i in range(2)]
        peer_in = sem("peer_in")
        sk_tr = sem("sk_tr")
        sk_T = sem("sk_T")

        a_cur = sem("a_cur")
        a_x1 = sem("a_x1")
        a_xtr = sem("a_xtr")
        a_xT = sem("a_xT")
        a_q = sem("a_q")
        a_qc = sem("a_qc")
        a_s = sem("a_s")
        a_sc = sem("a_sc")
        a_route = sem("a_route")
        a_diff = sem("a_diff")
        a_exp = sem("a_exp")
        a_dot = sem("a_dot")
        a_gelu = sem("a_gelu")
        a_coef = sem("a_coef")
        a_diag = sem("a_diag")
        a_pv = sem("a_pv")
        a_var = sem("a_var")
        a_std = sem("a_std")
        a_y = sem("a_y")
        a_yo = sem("a_yo")
        ch = sem("ch")
        tile_sems = [a_cur, a_x1, a_xtr, a_xT, a_q, a_qc, a_s, a_sc, a_route, a_diff, a_exp, a_dot,
                     a_gelu, a_coef, a_diag, a_pv, a_var, a_std, a_y, a_yo, ch]
        ended = {e: sem(f"ended_{e}") for e in ("pe", "act", "dve", "pool")}
        go = {e: sem(f"go_{e}") for e in ("pe", "act", "dve", "pool")}
        gu = [sem(f"gu{i}") for i in range(U_RING)]
        gv = [sem(f"gv{i}") for i in range(V_RING)]

        def rows(n):
            return P if n < PT else NS

        xp, xs = I["x_prompt"][0], I["x_sample"].rearrange("b t d -> (b t) d")

        def x_rows(n):
            return xp[n * P:(n + 1) * P, :] if n < PT else xs

        w_cols = I["w_in"][0].rearrange("(k p) c -> p k c", p=P)
        CHUNKS = [("k", c) for c in range(CT)] + [("q", c) for c in range(CT)]
        for c in range(CT):
            CHUNKS += [("a", c), ("g", c)]
        COL = {"q": 0, "k": AW, "a": 3 * AW, "g": 3 * AW + CC}
        GROUPS = [(0, 512), (512, 512), (SEQ, NS)]
        NPROJ = len(CHUNKS) * len(GROUPS)
        UNITS = [(t, h) for t in range(PT) for h in range(H)]

        block = ctx.enter_context(nc.Block())

        @block.sync
        def _(sp):
            sp.dma_start(ident[:, :], I["c_ident"]).then_inc(const_in, 16)
            for n in range(2):
                sp.dma_start(xt[:, n, :], x_rows(n)).then_inc(x_in[n], 16)
            sp.dma_start(cw[0:CK, :], I["conv_w"][0]).then_inc(aux_in, 16)
            for i, name in enumerate(("conv_b", "conv_ln_g", "conv_ln_b")):
                sp.dma_start(cw[CK + i:CK + i + 1, :], I[name]).then_inc(aux_in, 16)
            sp.dma_start(st_in[:, :, :], I["state_conv"][0].rearrange("(g b) r c -> (b r) g c", g=2)).then_inc(aux_in, 16)
            for c in range(W_RING):
                kind, i = CHUNKS[c]
                sp.dma_start(w_ring[:, c, :, :], w_cols[:, :, COL[kind] + i * P:COL[kind] + (i + 1) * P]).then_inc(w_in_s[c], 16)
            for n in range(2, TILES):
                sp.wait_ge(x_used, n - 1)
                sp.dma_start(xt[0:rows(n), n % 2, :], x_rows(n)).then_inc(x_in[n % 2], 16)
            sp.dma_start(bias_p[:, :], I["c_prompt_bias"]).then_inc(const_in, 16)
            sp.dma_start(bias_s[:, :], I["c_sample_bias"]).then_inc(const_in, 16)
            sp.dma_start(w_v[:, :, :], w_cols[:, :, 2 * AW:3 * AW]).then_inc(wv_in, 16)
            for c in range(W_RING, len(CHUNKS)):
                kind, i = CHUNKS[c]
                sp.wait_ge(proj_done, 3 * (c - W_RING + 1))
                sp.dma_start(w_ring[:, c % W_RING, :, :], w_cols[:, :, COL[kind] + i * P:COL[kind] + (i + 1) * P]).then_inc(w_in_s[c % W_RING], 16)
            for n in range(PT):
                sp.wait_ge(v_evac, n + 1)
                sp.dma_start(nv_p[0, 0].rearrange("t h e -> t (h e)")[n * P:(n + 1) * P, :], v[:, n, :]).then_inc(v_out, 16)
            sp.wait_ge(v_evac, TILES)
            for b in range(NB):
                sp.dma_start(nv_s[0, b, WIN - NT:WIN].rearrange("t h e -> t (h e)"), vs[b * NT:(b + 1) * NT, :]).then_inc(vn_out, 16)
            for n in range(ROWS_OUT):
                sp.wait_ge(row_evac, n + 1)
                if n < PT:
                    sp.dma_start(nk_p[0, 0].rearrange("t h e -> t (h e)")[n * P:(n + 1) * P, :], kst[:, n % 2, :]).then_inc(row_out[n % 2], 16)
                elif n == PT:
                    for b in range(NB):
                        sp.dma_start(nk_s[0, b, WIN - NT:WIN].rearrange("t h e -> t (h e)"), kst[b * NT:(b + 1) * NT, n % 2, :]).then_inc(row_out[n % 2], 16)
                elif n == PT + 1:
                    sp.dma_start(nc_p[0, 0], kst[0:PAST, n % 2, :]).then_inc(row_out[n % 2], 16)
                else:
                    for b in range(NB):
                        sp.dma_start(nc_s[0, b, PAST - NT:PAST, :], kst[b * NT:(b + 1) * NT, n % 2, :]).then_inc(row_out[n % 2], 16)
            for b in range(NB):
                for new, old in ((nk_s, I["cache_k_win"]), (nv_s, I["cache_v_win"])):
                    sp.dma_start(new[0, b, 0:WIN - NT].rearrange("t h e -> (t h e)").rearrange("(a m) -> a m", a=256),
                                 old[0, b, NT:WIN].rearrange("t h e -> (t h e)").rearrange("(a m) -> a m", a=256)).then_inc(out_dma, 16)
            sp.dma_start(nc_s[0, :, 0:PAST - NT, :], I["state_conv"][0, :, NT:PAST, :]).then_inc(out_dma, 16)

            def load_cache(cache, b, dst, arrived):
                src = cache[0, b].rearrange("t h e -> t (h e)")
                sp.dma_start(dst[0:NFAR, 0:FSL, :], src[0:FAR, :].rearrange("(g r) c -> g r c", r=16)[:, 0:FSL, :]).then_inc(arrived, 16)
                sp.dma_start(dst[:, FSL:, :], src[FAR:WIN, :].rearrange("(p s) c -> p s c", s=LSL)).then_inc(arrived, 16)

            sp.wait_ge(proj_done, NPROJ)
            sp.wait_ge(v_done, TILES)
            load_cache(I["cache_k_win"], 1, k_cache[1], kc_in[1])
            sp.wait_ge(pv_done, len(UNITS))
            sp.wait_ge(v_out, 16 * PT)
            load_cache(I["cache_k_win"], 0, k_cache[0], kc_in[0])
            load_cache(I["cache_v_win"], 0, v_cache, vc_in)
            sp.wait_ge(vn_out, 16 * NB)
            sp.wait_ge(cv, 2 * CK * CT)
            sp.dma_start(v_new[:, :, :], nv_s[0, :, WIN - NT:WIN].rearrange("b t h e -> t b (h e)")).then_inc(vn_in, 16)
            for b in range(1, NB):
                if b + 1 < NB:
                    sp.wait_ge(kc_tr, b * CT * 3)
                    load_cache(I["cache_k_win"], b + 1, k_cache[(b + 1) % 2], kc_in[(b + 1) % 2])
                sp.wait_ge(spv_done, b)
                load_cache(I["cache_v_win"], b, v_cache, vc_in)
            sp.wait_ge(kc_tr, NB * CT * 3)
            sp.dma_start(w_out[:, :, :], I["w_out"][0].rearrange("(k p) n -> p k n", p=P)).then_inc(wout_in, 16)
            sp.wait_ge(spv_done, NB)
            sp.dma_start(wq[:, :, :], I["w_query"][0].rearrange("(k p) n -> p k n", p=P)).then_inc(peer_in, 16)
            for i, name in enumerate(("ln1_g", "ln1_b")):
                sp.dma_start(lnw[:, i, :], I[name].partition_broadcast(P)).then_inc(lnw_in, 16)
            for n in range(TILES):
                if n >= 2:
                    sp.wait_ge(res_done, n - 1)
                sp.dma_start(xr[0:rows(n), n % 2, :], x_rows(n)).then_inc(xr_in[n % 2], 16)
                if n:
                    sp.wait_ge(x1_done, n)
                    sp.dma_start(x1_d[(n - 1) * P:n * P, :], x1o[:, (n - 1) % 2, :]).then_inc(x1_out[(n - 1) % 2], 16)
            sp.wait_ge(x1_done, TILES)
            sp.dma_start(x1_d[PT * P:PT * P + NS, :], x1o[0:NS, PT % 2, :]).then_inc(x1_out[PT % 2], 16)
            sp.dma_start(x1_d[PT * P + NS:TILES * P, :], x1o[0:NS, PT % 2, :]).then_inc(x1_out[PT % 2], 16)
            sp.wait_ge(x1_out[0], 16 * 6)
            sp.wait_ge(x1_out[1], 16 * 4)
            sp.wait_ge(mix_done, TILES)
            for i in range(2 * PH):
                sp.dma_start(sk_in[:, i, :], I["sub_keys"][0, i // 2, i % 2]).then_inc(peer_in, 16)
            sp.dma_start(iden2[:, :], I["c_ident"]).then_inc(peer_in, 16)
            sp.dma_start(iota[:, :], I["c_iota"]).then_inc(peer_in, 16)
            for i, name in enumerate(("ln2_g", "ln2_b")):
                sp.dma_start(lnw2[:, i, :], I[name].partition_broadcast(P)).then_inc(peer_in, 16)
            sp.dma_start(x1n[:, :], x1_d[0:P, :]).then_inc(a_x1, 16)

            def between(last=False):
                for e in ended.values():
                    sp.wait_ge(e, 1)
                for s in [*tile_sems, *ended.values()]:
                    sp.sem_clear(s)
                for s in go.values():
                    sp.sem_inc(s, 1)

            between()
            with sp.Fori(0, PT) as n:
                sp.wait_ge(a_cur, 1)
                sp.dma_start(x1n[:, :], x1_d[bass.ds(n * P + P, P), :]).then_inc(a_x1, 16)
                sp.wait_ge(a_y, 1)
                sp.dma_start(y_p[0][bass.ds(n * P, P), :], yt[:, :]).then_inc(a_yo, 16)
                sp.wait_ge(a_yo, 16)
                between()
            sp.wait_ge(a_y, 1)
            sp.dma_start(y_s.rearrange("b t d -> (b t) d"), yt[0:NS, :]).then_inc(a_yo, 16)
            sp.wait_ge(a_yo, 16)
            sp.wait_ge(out_dma, 16 * (2 * NB + 1))
            sp.wait_ge(v_out, 16 * PT)
            sp.wait_ge(row_out[0], 16 * (PT // 2 + NB + NB))
            sp.wait_ge(row_out[1], 16 * (PT // 2 + 1))

        @block.gpsimd
        def _(pool):
            def gathers(nrow):
                pool.wait_ge(a_cur, 1)
                for s in range(SLOTS + TOP):
                    if s < SLOTS:
                        if s >= U_RING:
                            pool.wait_ge(a_dot, s - U_RING + 1)
                        pool.indirect_dma_start(u_buf[0:nrow, s % U_RING, :], None, I["expert_u"][0],
                                                bass.IndirectOffsetOnAxis(ap=idc[0:nrow, s:s + 1], axis=0)).then_inc(gu[s % U_RING], 16)
                    r = s - TOP
                    if r >= 0:
                        if r >= V_RING:
                            pool.wait_ge(a_pv, r - V_RING + 1)
                        pool.indirect_dma_start(v_buf[0:nrow, r % V_RING, :], None, I["expert_v"][0],
                                                bass.IndirectOffsetOnAxis(ap=idc[0:nrow, r:r + 1], axis=0)).then_inc(gv[r % V_RING], 16)

            def end_tile():
                pool.sem_inc(ended["pool"], 1)
                pool.wait_ge(go["pool"], 1)
                pool.sem_clear(go["pool"])

            end_tile()
            with pool.Fori(0, PT) as n:
                gathers(P)
                end_tile()
            gathers(NS)

        @block.scalar
        def _(act):
            act.wait_ge(aux_tr, 1)
            act.activation(cwT[:, :, :], bank[4][:, 0:CT * (CK + 3)].rearrange("p (c k) -> p c k", c=CT), ACT.Copy).then_inc(aux_ready, 1)
            for g in range(2):
                act.wait_ge(aux_tr, 2 + g)
                act.activation(gluS[:, :, g * 4:g * 4 + 4, 0:PAST],
                               bank[5 + g][:, 0:CT * 120].rearrange("p (c b r) -> p c b r", c=CT, b=4), ACT.Copy).then_inc(aux_ready, 1)
            for n in range(TILES):
                act.wait_ge(x_used, n + 1)
                for half in range(2):
                    act.activation(xT[:, half * 4:half * 4 + 4, n * P:n * P + rows(n)],
                                   bank[2 * (n % 2) + half][:, :].rearrange("p (k t) -> p k t", k=4)[:, :, 0:rows(n)], ACT.Copy).then_inc(xT_ready, 1)
            ng = 0
            for c, (kind, i) in enumerate(CHUNKS):
                for g, (t0, tn) in enumerate(GROUPS):
                    j = 3 * c + g
                    act.wait_ge(proj_done, j + 1)
                    src = bank[4 + j % 4][:, 0:tn]
                    if kind in "qk":
                        full, new = (qT, qTs) if kind == "q" else (kT, kTs)
                        dst = full[:, i, t0:t0 + tn] if g < 2 else new[:, i, :]
                        act.activation(dst, src, ACT.Copy).then_inc(proj_evac, 1)
                    elif kind == "a":
                        dst = gluP[:, i, PAST + t0:PAST + t0 + tn] if g < 2 else glu_new[:, i, :]
                        act.activation(dst, src, ACT.Copy).then_inc(proj_evac, 1)
                    else:
                        if ng >= 2:
                            act.wait_ge(glu_done, ng - 1)
                        act.activation(sig[:, ng % 2, 0:tn], src, ACT.Sigmoid).then_inc(proj_evac, 1)
                        ng += 1
            for n in range(ROWS_OUT):
                act.wait_ge(row_tr, n + 1)
                if n in (2, 3, 4, 5, 6, 7, 8, 9, 10):
                    before = (n - 2) // 2 + 1
                    act.wait_ge(row_out[n % 2], 16 * (before if n < 10 else PT // 2 + NB))
                m = P if n < PT else NS if n in (PT, PT + 2) else PAST
                act.activation(kst[0:m, n % 2, :], bank[n % 4][0:m, :], ACT.Copy).then_inc(row_evac, 1)
            for i, (t, h) in enumerate(UNITS):
                L = (t + 1) * P
                act.wait_ge(nm_done, i + 1)
                act.activation(sm[:, i % 2, 0:L], sm[:, i % 2, 0:L], ACT.Exp, bias=small[:, 2 + i % 2:3 + i % 2], scale=SCALE,
                               accum_out=small[:, 4 + i % 2:5 + i % 2]).then_inc(exp_done, 1)
                act.wait_ge(p_tr, i + 1)
                if i >= 2:
                    act.wait_ge(pv_done, i - 1)
                act.activation(pT[:, i % 2, 0:L], psum[:, 4 * 512:4 * 512 + L], ACT.Copy).then_inc(pT_ready, 1)
                if (h == 0 and t) or i == len(UNITS) - 1:
                    d = t if i == len(UNITS) - 1 else t - 1
                    act.wait_ge(att_tr, d + 1)
                    act.activation(mixedT[:, 0:CT, d * P:(d + 1) * P], bank[7].rearrange("p (c q) -> p c q", c=CT), ACT.Copy).then_inc(att_T, 1)
            def keys_T(b):
                for c in range(CT):
                    for part in range(3):
                        act.wait_ge(kc_tr, (b * CT + c) * 3 + part + 1)
                        if b and c == 0 and part == 0:
                            act.wait_ge(ss_done, b)
                        w = HALF if part < 2 else LSL * P
                        act.activation(kTc[:, c, part * HALF:part * HALF + w], bank[part][:, 0:w], ACT.Copy).then_inc(kc_evac, 1)

            keys_T(0)
            for b in range(NB):
                act.wait_ge(snm_done, b + 1)
                act.activation(sms[:, :], sms[:, :], ACT.Exp, bias=small[0:NS, 8:9], scale=SCALE, accum_out=small[0:NS, 9:10]).then_inc(sexp_done, 1)
                if b + 1 < NB:
                    keys_T(b + 1)
                act.wait_ge(sp_tr, b + 1)
                if b:
                    act.wait_ge(spv_done, b)
                act.activation(pTs[0:NFAR, 0:FSL, :], bank[7][0:NFAR, :].rearrange("p (s q) -> p s q", s=FSL), ACT.Copy).then_inc(spT_ready, 1)
                act.activation(pTs[:, FSL:FSL + LSL, :], bank[3][:, 0:LSL * NS].rearrange("p (s q) -> p s q", s=LSL), ACT.Copy).then_inc(spT_ready, 1)
                act.activation(pTs[0:NT, FSL + LSL, :], bank[3][0:NT, LSL * NS:(LSL + 1) * NS], ACT.Copy).then_inc(spT_ready, 1)
                act.wait_ge(spv_done, b + 1)
                out = bank[3][:, O_PV:O_PV + CT * 2 * NT].rearrange("p (c u) -> p c u", c=CT)
                for u in range(2):
                    act.activation(mixedT[u * E:(u + 1) * E, 0:CT, SEQ + b * NT:SEQ + (b + 1) * NT],
                                   out[u * E:(u + 1) * E, :, u * NT:(u + 1) * NT], ACT.Copy).then_inc(satt_T, 1)
            for n in range(TILES):
                act.wait_ge(c_var, n + 1)
                act.activation(cstat[0:rows(n), n % 2, 9:10], cstat[0:rows(n), n % 2, 8:9], ACT.Sqrt).then_inc(c_std, 1)
                act.wait_ge(c_tr2, n + 1)
                for c in range(CT):
                    act.activation(mixedT[:, CT + c, n * P:n * P + rows(n)], bank[2 + n % 2][:, c * P:c * P + rows(n)], ACT.Silu,
                                   bias=cwT[:, c, CK + 2:CK + 3], scale=cwT[:, c, CK + 1:CK + 2]).then_inc(c_T, 1)
            for n in range(TILES):
                act.wait_ge(l_var, n + 1)
                act.activation(stat[0:rows(n), n % 2, 17:18], stat[0:rows(n), n % 2, 16:17], ACT.Sqrt).then_inc(l_std, 1)
            for g in range(4):
                act.wait_ge(sk_tr, g + 1)
                act.activation(skT[:, 4 * g:4 * g + 4, :], bank[g][:, :].rearrange("p (s k) -> p s k", s=4), ACT.Copy).then_inc(sk_T, 1)

            def x1_transposed():
                for half in range(2):
                    act.wait_ge(a_xtr, half + 1)
                    act.activation(x1T[:, half * 4:half * 4 + 4, :], bank[2 + half][:, :].rearrange("p (k t) -> p k t", k=4), ACT.Copy).then_inc(a_xT, 1)

            def route_copies(h):
                act.wait_ge(a_q, h + 1)
                act.activation(qh[:, h % 2, :], bank[4 + h % 2][:, 0:2 * P], ACT.Copy).then_inc(a_qc, 1)
                act.wait_ge(a_s, h + 1)
                if h >= 2:
                    act.wait_ge(a_route, h - 1)
                act.activation(sh[:, h % 2, :], bank[6 + h % 2][:, 0:2 * NK], ACT.Copy).then_inc(a_sc, 1)

            def gate_exp(h):
                act.wait_ge(a_diff, h + 1)
                act.activation(ex[:, h % 2, :], ex[:, h % 2, :], ACT.Exp, accum_out=den[:, h % 2:h % 2 + 1]).then_inc(a_exp, 1)

            def diags(h):
                act.wait_ge(a_coef, h + 1)
                for k in range(h * TOP, (h + 1) * TOP):
                    if k >= DG_RING:
                        act.wait_ge(a_pv, k - DG_RING + 1)
                    act.activation(diag[:, k % DG_RING, :], iden2[:, :], ACT.Copy, scale=coef[:, k:k + 1]).then_inc(a_diag, 1)

            def tile(nrow, route):
                if route:
                    x1_transposed()
                for h in range(PH + 1):
                    if route and h < PH:
                        route_copies(h)
                    if h:
                        diags(h - 1)
                    if h < PH:
                        act.wait_ge(a_dot, (h + 1) * TOP)
                        act.activation(gel[0:nrow, h * TOP:(h + 1) * TOP], dots[0:nrow, h * TOP:(h + 1) * TOP], ACT.Gelu).then_inc(a_gelu, 1)
                        if route:
                            gate_exp(h)
                act.wait_ge(a_var, 1)
                act.activation(st2[0:nrow, 17:18], st2[0:nrow, 16:17], ACT.Sqrt).then_inc(a_std, 1)

            def end_tile(last=a_std, value=1):
                act.wait_ge(last, value)
                act.sem_inc(ended["act"], 1)
                act.wait_ge(go["act"], 1)
                act.sem_clear(go["act"])

            x1_transposed()
            for h in range(PH):
                route_copies(h)
                gate_exp(h)
            act.wait_ge(a_route, PH)
            end_tile(a_exp, PH)
            with act.Fori(0, PT) as n:
                tile(P, True)
                end_tile()
            tile(NS, False)

        @block.vector
        def _(dve):
            steps = [0]

            def seq(ins, s=dv):
                steps[0] += 1
                ins.then_inc(s, 1)
                dve.wait_ge(s, steps[0])

            for c in range(CT):
                dve.memset(gluP[:, c, 0:PAST], 0.0).then_inc(pads, 1)
            ng = 0
            for i in range(CT):
                for g, (t0, tn) in enumerate(GROUPS):
                    dve.wait_ge(proj_evac, 3 * (2 * CT + 2 * i + 1) + g + 1)
                    dst = gluP[:, i, PAST + t0:PAST + t0 + tn] if g < 2 else glu_new[:, i, :]
                    dve.tensor_tensor(dst, dst, sig[:, ng % 2, 0:tn], ALU.mult).then_inc(glu_done, 1)
                    ng += 1
            dve.wait_ge(glu_done, ng)
            dve.wait_ge(aux_ready, 3)
            for c in range(CT):
                dve.tensor_copy(gluS[:, c, :, PAST:], glu_new[:, c, :].rearrange("p (b t) -> p b t", b=NB)).then_inc(glu_s, 1)
            for n in range(TILES):
                dve.wait_ge(v_done, n + 1)
                dst = v[:, n, :] if n < PT else vs[:, :]
                dve.tensor_copy(dst, bank[4 + (NPROJ + n) % 4][0:rows(n), :]).then_inc(v_evac, 1)
            dve.wait_ge(pads, CT)
            dve.wait_ge(glu_s, CT)
            dve.wait_ge(vn_out, 16 * NB)
            taps = [(k, c, s) for k in range(CK) for c in range(CT) for s in range(2)]

            def tap(m):
                k, c, s = taps[m]
                if s == 0:
                    src, dst = gluP[:, c, k:k + SEQ], conv[:, c, 0:SEQ]
                else:
                    src, dst = gluS[:, c, :, k:k + NT], conv[:, c, SEQ:TOK].rearrange("p (b t) -> p b t", b=NB)
                w = cwT[:, c, k:k + 1]
                if k == 0:
                    dve.tensor_scalar(dst, src, w, cwT[:, c, CK:CK + 1], ALU.mult, ALU.add).then_inc(cv, 1)
                else:
                    dve.wait_ge(cv, m - 2 * CT + 1)
                    dve.scalar_tensor_tensor(dst, src, w, dst, ALU.mult, ALU.add).then_inc(cv, 1)

            def normalise(i):
                t, h = UNITS[i]
                dve.wait_ge(exp_done, i + 1)
                seq(dve.reciprocal(small[:, 6:7], small[:, 4 + i % 2:5 + i % 2]))
                dve.wait_ge(pv_done, i + 1)
                if h == 0 and t >= 2:
                    dve.wait_ge(att_tr, t - 1)
                dve.tensor_scalar(att[:, t % 2, h * E:(h + 1) * E], bank[6 + i % 2][:, 0:E], small[:, 6:7], None, ALU.mult).then_inc(att_done, 1)
                dve.wait_ge(att_done, i + 1)

            dve.wait_ge(const_in, 48)
            m = 0
            for i, (t, h) in enumerate(UNITS):
                L = (t + 1) * P
                dve.wait_ge(s_done, i + 1)
                if i >= 2:
                    dve.wait_ge(p_tr, i - 1)
                off = SEQ - L
                s0 = 2 * (i % 2) * 512
                seq(dve.tensor_tensor_reduce(out=sm[:, i % 2, 0:L], in0=psum[:, s0:s0 + L], in1=bias_p[:, off:SEQ], scale=1.0, scalar=LOWEST,
                                             op0=ALU.add, op1=ALU.max, accum_out=small[:, i % 2:i % 2 + 1]))
                dve.tensor_scalar(small[:, 2 + i % 2:3 + i % 2], small[:, i % 2:i % 2 + 1], -SCALE, None, ALU.mult).then_inc(nm_done, 1)
                for _ in range(4):
                    if m < len(taps):
                        tap(m)
                        m += 1
                if i:
                    normalise(i - 1)
            normalise(len(UNITS) - 1)
            while m < len(taps):
                tap(m)
                m += 1
            dve.wait_ge(pT_ready, len(UNITS))
            dve.wait_ge(x_used, TILES)
            seq(dve.memset(qbd[:, :, :, :], 0.0))
            for c in range(CT):
                for u in range(2):
                    hh = 2 * c + u
                    dve.tensor_copy(qbd[u * E:(u + 1) * E, c, :, hh * NT:(hh + 1) * NT],
                                    qTs[u * E:(u + 1) * E, c, :].rearrange("p (b t) -> p b t", b=NB)).then_inc(qbd_done, 1)
            for b in range(NB):
                dve.wait_ge(ss_done, b + 1)
                for lo, hi, bk in ((0, C_FAR2, 0), (C_FAR2, C_NEAR, 1), (C_NEAR, KEYS, 2)):
                    seq(dve.tensor_tensor(sms[:, lo:hi], bank[SB[bk]][0:NS, 0:hi - lo], bias_s[:, lo:hi], ALU.add))
                seq(dve.reduce_max(small[0:NS, 7:8], sms[:, :], AX.X))
                dve.tensor_scalar(small[0:NS, 8:9], small[0:NS, 7:8], -SCALE, None, ALU.mult).then_inc(snm_done, 1)
                dve.wait_ge(sexp_done, b + 1)
                seq(dve.reciprocal(small[0:NS, 10:11], small[0:NS, 9:10]))
                dve.tensor_scalar(sms[:, :], sms[:, :], small[0:NS, 10:11], None, ALU.mult).then_inc(sp_done, 1)
            for n in range(TILES):
                m_, s_ = rows(n), cstat[0:rows(n), n % 2, :]
                dve.wait_ge(c_tr, n + 1)
                seq(dve.bn_stats(s_[:, 0:6], bank[n % 2][0:m_, :]))
                seq(dve.bn_aggr(s_[:, 6:8], s_[:, 0:6]))
                dve.tensor_scalar(s_[:, 8:9], s_[:, 7:8], EPS, None, ALU.add).then_inc(c_var, 1)
                dve.wait_ge(c_std, n + 1)
                seq(dve.reciprocal(s_[:, 10:11], s_[:, 9:10]))
                if n >= 2:
                    dve.wait_ge(c_tr2, n - 1)
                dve.tensor_scalar(cn[0:m_, n % 2, :], bank[n % 2][0:m_, :], s_[:, 6:7], s_[:, 10:11], ALU.subtract, ALU.mult).then_inc(c_norm, 1)
            dve.wait_ge(lnw_in, 32)
            for n in range(TILES):
                m_, s_ = rows(n), stat[0:rows(n), n % 2, :]
                r_ = res[0:m_, n % 2, :]
                dve.wait_ge(mix_done, n + 1)
                dve.wait_ge(xr_in[n % 2], 16 * (n // 2 + 1))
                b0 = 4 * (n % 2)
                for half in range(2):
                    sl = slice(half * 512, half * 512 + 512)
                    seq(dve.scalar_tensor_tensor(r_[:, sl], xr[0:m_, n % 2, sl], ALPHA, bank[b0 + half][0:m_, :], ALU.mult, ALU.add))
                    seq(dve.bn_stats(s_[:, 6 * half:6 * half + 6], r_[:, sl]))
                dve.sem_inc(res_done, 1)
                seq(dve.bn_aggr(s_[:, 12:14], s_[:, 0:12]))
                dve.tensor_scalar(s_[:, 16:17], s_[:, 13:14], EPS, None, ALU.add).then_inc(l_var, 1)
                dve.wait_ge(l_std, n + 1)
                seq(dve.reciprocal(s_[:, 18:19], s_[:, 17:18]))
                seq(dve.tensor_scalar(r_, r_, s_[:, 12:13], s_[:, 18:19], ALU.subtract, ALU.mult))
                seq(dve.tensor_tensor(r_, r_, lnw[0:m_, 0, :], ALU.mult))
                if n >= 2:
                    dve.wait_ge(x1_out[n % 2], 16 * (n // 2))
                dve.tensor_tensor(x1o[0:m_, n % 2, :], r_, lnw[0:m_, 1, :], ALU.add).then_inc(x1_done, 1)

            local = [0]

            def step(ins):
                local[0] += 1
                ins.then_inc(ch, 1)
                dve.wait_ge(ch, local[0])

            def best(vals, idx, scores, spare):
                step(dve.max(vals[:, 0:8], scores))
                step(dve.match_replace(spare, vals[:, 0:8], scores, LOWEST))
                step(dve.max(vals[:, 8:16], spare))
                step(dve.max_index(idx[:, 0:8], vals[:, 0:8], scores))
                step(dve.max_index(idx[:, 8:16], vals[:, 8:16], spare))

            def route(h):
                dve.wait_ge(a_sc, h + 1)
                for side in range(2):
                    best(tv[:, side, :], ti[:, side, :], sh[:, h % 2, side * NK:(side + 1) * NK], s2[:, side, :])
                step(dve.tensor_copy(tif[:, :, :], ti[:, :, :]))
                step(dve.tensor_tensor(cand[:, :].rearrange("p (a b) -> p a b", a=TOP),
                                       tv[:, 0, :].unsqueeze(2).broadcast_to([P, TOP, TOP]),
                                       tv[:, 1, :].unsqueeze(1).broadcast_to([P, TOP, TOP]), ALU.add))
                best(bv[:, :], bj[:, :], cand[:, :], cand2[:, :])
                step(dve.tensor_scalar(ex[:, h % 2, :], bv[:, :], bv[:, 0:1], None, ALU.subtract))
                dve.sem_inc(a_diff, 1)
                step(dve.tensor_scalar(ab[:, 0, :], bj[:, :], 4, None, ALU.logical_shift_right))
                step(dve.tensor_scalar(ab[:, 1, :], bj[:, :], 15, None, ALU.bitwise_and))
                step(dve.tensor_copy(abf[:, :, :], ab[:, :, :]))
                for side in range(2):
                    e3 = eq[:, side, :].rearrange("p (k r) -> p k r", k=TOP)
                    step(dve.tensor_tensor(e3, abf[:, side, :].unsqueeze(2).broadcast_to([P, TOP, TOP]),
                                           iota[:, :].unsqueeze(1).broadcast_to([P, TOP, TOP]), ALU.is_equal))
                    step(dve.tensor_tensor(e3, e3, tif[:, side, :].unsqueeze(1).broadcast_to([P, TOP, TOP]), ALU.mult))
                    step(dve.reduce_sum(eif[:, side, :], e3, AX.X))
                step(dve.scalar_tensor_tensor(idn[:, h * TOP:(h + 1) * TOP], eif[:, 0, :], float(NK), eif[:, 1, :], ALU.mult, ALU.add))
                dve.wait_ge(a_exp, h + 1)
                step(dve.reciprocal(rdn[:, h % 2:h % 2 + 1], den[:, h % 2:h % 2 + 1]))
                step(dve.tensor_scalar(gtn[:, h * TOP:(h + 1) * TOP], ex[:, h % 2, :], rdn[:, h % 2:h % 2 + 1], None, ALU.mult))
                dve.sem_inc(a_route, 1)

            def tile(nrow, with_route, base_of):
                m_ = nrow
                step(dve.tensor_copy(x1c[:, :], x1n[:, :]))
                step(dve.tensor_copy(idc[:, :], idn[:, :]))
                step(dve.tensor_copy(gtc[:, :], gtn[:, :]))
                dve.sem_inc(a_cur, 1)
                for h in range(PH):
                    for k in range(h * TOP, (h + 1) * TOP):
                        if k >= 2:
                            dve.wait_ge(a_dot, k - 1)
                        dve.wait_ge(gu[k % U_RING], base_of(k))
                        dve.tensor_tensor_reduce(out=junk[0:m_, k % 2, :], in0=u_buf[0:m_, k % U_RING, :], in1=x1c[0:m_, :], scale=1.0,
                                                 scalar=0.0, op0=ALU.mult, op1=ALU.add, accum_out=dots[0:m_, k:k + 1]).then_inc(a_dot, 1)
                    if with_route:
                        route(h)
                    dve.wait_ge(a_gelu, h + 1)
                    hs = slice(h * TOP, (h + 1) * TOP)
                    dve.tensor_tensor(coef[0:m_, hs], gel[0:m_, hs], gtc[0:m_, hs], ALU.mult).then_inc(a_coef, 1)
                dve.wait_ge(a_pv, SLOTS)
                dve.wait_ge(a_dot, SLOTS)
                r_, s_ = junk[0:m_, 0, :], st2[0:m_, :]
                for half in range(2):
                    sl = slice(half * 512, half * 512 + 512)
                    step(dve.scalar_tensor_tensor(r_[:, sl], x1c[0:m_, sl], ALPHA, bank[half][0:m_, :], ALU.mult, ALU.add))
                    step(dve.bn_stats(s_[:, 6 * half:6 * half + 6], r_[:, sl]))
                step(dve.bn_aggr(s_[:, 12:14], s_[:, 0:12]))
                dve.tensor_scalar(s_[:, 16:17], s_[:, 13:14], EPS, None, ALU.add).then_inc(a_var, 1)
                dve.wait_ge(a_std, 1)
                step(dve.reciprocal(s_[:, 18:19], s_[:, 17:18]))
                step(dve.tensor_scalar(r_, r_, s_[:, 12:13], s_[:, 18:19], ALU.subtract, ALU.mult))
                step(dve.tensor_tensor(r_, r_, lnw2[0:m_, 0, :], ALU.mult))
                dve.tensor_tensor(yt[0:m_, :], r_, lnw2[0:m_, 1, :], ALU.add).then_inc(a_y, 1)

            def end_tile(last=a_y, value=1):
                dve.wait_ge(last, value)
                dve.sem_inc(ended["dve"], 1)
                dve.wait_ge(go["dve"], 1)
                dve.sem_clear(go["dve"])
                local[0] = 0

            dve.wait_ge(peer_in, 16 * (5 + 2 * PH))
            for h in range(PH):
                route(h)
            end_tile(a_route, PH)
            with dve.Fori(0, PT) as n:
                tile(P, True, lambda k: n * (16 * SLOTS // U_RING) + 16 * (k // U_RING + 1))
                end_tile()
            tile(NS, False, lambda k: PT * (16 * SLOTS // U_RING) + 16 * (k // U_RING + 1))

        @block.tensor
        def _(pe):
            pe.wait_ge(const_in, 16)
            pe.wait_ge(aux_in, 16 * 5)
            for c in range(CT):
                last = pe.transpose(bank[4][:, c * (CK + 3):(c + 1) * (CK + 3)], cw[0:CK + 3, c * P:(c + 1) * P], ident[0:CK + 3, 0:CK + 3])
            last.then_inc(aux_tr, 1)
            for g in range(2):
                for c in range(CT):
                    last = pe.transpose(bank[5 + g][:, c * 120:(c + 1) * 120], st_in[0:120, g, c * P:(c + 1) * P], ident[0:120, 0:120])
                last.then_inc(aux_tr, 1)
            for n in range(TILES):
                pe.wait_ge(x_in[n % 2], 16 * (n // 2 + 1))
                if n >= 2:
                    pe.wait_ge(xT_ready, 2 * (n - 1))
                for k in range(KD):
                    last = pe.transpose(bank[2 * (n % 2) + k // 4][:, k % 4 * P:k % 4 * P + rows(n)], xt[0:rows(n), n % 2, k * P:(k + 1) * P],
                                        ident[0:rows(n), 0:rows(n)])
                last.then_inc(x_used, 1)
            pe.wait_ge(xT_ready, 2 * TILES)
            pe.wait_ge(aux_ready, 3)
            for c in range(len(CHUNKS)):
                pe.wait_ge(w_in_s[c % W_RING], 16 * (c // W_RING + 1))
                for g, (t0, tn) in enumerate(GROUPS):
                    j = 3 * c + g
                    if j >= 4:
                        pe.wait_ge(proj_evac, j - 3)
                    for k in range(KD):
                        last = pe.matmul(bank[4 + j % 4][:, 0:tn], w_ring[:, c % W_RING, k, :], xT[:, k, t0:t0 + tn], start=(k == 0), stop=(k == KD - 1))
                    last.then_inc(proj_done, 1)
            pe.wait_ge(wv_in, 16)
            for n in range(TILES):
                if n < 4:
                    pe.wait_ge(proj_evac, NPROJ - 3 + n)
                else:
                    pe.wait_ge(v_evac, n - 3)
                for k in range(KD):
                    last = pe.matmul(bank[4 + (NPROJ + n) % 4][0:rows(n), :], xT[:, k, n * P:n * P + rows(n)], w_v[:, k, :], start=(k == 0), stop=(k == KD - 1))
                last.then_inc(v_done, 1)
            pe.wait_ge(glu_done, 3 * CT)
            for n in range(ROWS_OUT):
                if n >= 4:
                    pe.wait_ge(row_evac, n - 3)
                for c in range(CT):
                    if n < PT:
                        src, m = kT[:, c, n * P:(n + 1) * P], P
                    elif n == PT:
                        src, m = kTs[:, c, :], NS
                    elif n == PT + 1:
                        src, m = gluP[:, c, SEQ:SEQ + PAST], PAST
                    else:
                        src, m = glu_new[:, c, :], NS
                    last = pe.transpose(bank[n % 4][0:m, c * P:(c + 1) * P], src, ident[:, :])
                last.then_inc(row_tr, 1)
            pe.wait_ge(row_evac, ROWS_OUT)
            pe.wait_ge(v_evac, TILES)

            def scores(i):
                t, h = UNITS[i]
                c, r = h // 2, E * (h % 2)
                L = (t + 1) * P
                if i >= 2:
                    pe.wait_ge(nm_done, i - 1)
                for half in range(0, (L + 511) // 512):
                    w = min(512, L - half * 512)
                    last = pe.matmul(bank[2 * (i % 2) + half][:, 0:w], qT[r:r + E, c, t * P:(t + 1) * P], kT[r:r + E, c, half * 512:half * 512 + w],
                                     start=True, stop=True)
                last.then_inc(s_done, 1)

            def weights_T(i):
                t, h = UNITS[i]
                pe.wait_ge(exp_done, i + 1)
                if i:
                    pe.wait_ge(pT_ready, i)
                for j in range(t + 1):
                    last = pe.transpose(bank[4 + j // 4][:, j % 4 * P:(j % 4 + 1) * P], sm[:, i % 2, j * P:(j + 1) * P], ident[:, :])
                last.then_inc(p_tr, 1)

            def values(i):
                t, h = UNITS[i]
                pe.wait_ge(pT_ready, i + 1)
                if i >= 2:
                    pe.wait_ge(att_done, i - 1)
                if h == 1 and t:
                    pe.wait_ge(att_T, t)
                for j in range(t + 1):
                    last = pe.matmul(bank[6 + i % 2][:, 0:E], pT[:, i % 2, j * P:(j + 1) * P], v[:, j, h * E:(h + 1) * E], start=(j == 0), stop=(j == t))
                last.then_inc(pv_done, 1)

            def att_transposes(t):
                pe.wait_ge(att_done, (t + 1) * H)
                for c in range(CT):
                    last = pe.transpose(bank[7][:, c * P:(c + 1) * P], att[:, t % 2, c * P:(c + 1) * P], ident[:, :])
                last.then_inc(att_tr, 1)

            scores(0)
            for i in range(len(UNITS)):
                if i + 1 < len(UNITS):
                    scores(i + 1)
                if i:
                    values(i - 1)
                weights_T(i)
                if i and i % H == 0:
                    att_transposes(i // H - 1)
            values(len(UNITS) - 1)
            att_transposes(PT - 1)
            pe.wait_ge(att_T, PT)
            pe.wait_ge(qbd_done, 2 * CT)
            pe.wait_ge(vn_in, 16)
            def keys_transposes(b):
                pe.wait_ge(kc_in[b % 2], 32 * (b // 2 + 1))
                for c in range(CT):
                    for part in range(3):
                        if b or c:
                            pe.wait_ge(kc_evac, (b * CT + c - 1) * 3 + part + 1)
                        for s in range(4):
                            if part < 2:
                                last = pe.transpose(bank[part][:, s * NFAR:(s + 1) * NFAR], k_cache[b % 2][0:NFAR, part * 4 + s, c * P:(c + 1) * P], ident[0:NFAR, 0:NFAR])
                            else:
                                last = pe.transpose(bank[part][:, s * P:(s + 1) * P], k_cache[b % 2][:, FSL + s, c * P:(c + 1) * P], ident[:, :])
                        last.then_inc(kc_tr, 1)

            def sample_scores(b):
                pe.wait_ge(kc_evac, (b + 1) * CT * 3)
                if b:
                    pe.wait_ge(snm_done, b)
                for part in range(3):
                    o = bank[SB[part]]
                    w = HALF if part < 2 else LSL * P
                    for c in range(CT):
                        last = pe.matmul(o[0:NS, 0:w], qbd[:, c, b, :], kTc[:, c, part * HALF:part * HALF + w], start=(c == 0), stop=(c == CT - 1))
                    if part == 0:
                        for c in range(CT):
                            last = pe.matmul(o[0:NS, HALF:HALF + NT], qbd[:, c, b, :], kTs[:, c, b * NT:(b + 1) * NT], start=(c == 0), stop=(c == CT - 1))
                last.then_inc(ss_done, 1)

            def sample_weights_T(b):
                pe.wait_ge(sp_done, b + 1)
                if b:
                    pe.wait_ge(spT_ready, 3 * b)
                    pe.wait_ge(satt_T, 2 * b)
                for s in range(FSL + LSL + 1):
                    if s < FSL:
                        col, m = (s * NFAR if s < 4 else C_FAR2 + (s - 4) * NFAR), NFAR
                        o = bank[7][0:NFAR, s * NS:(s + 1) * NS]
                    elif s < FSL + LSL:
                        col, m = C_NEAR + (s - FSL) * P, P
                        o = bank[3][:, (s - FSL) * NS:(s - FSL + 1) * NS]
                    else:
                        col, m = C_NEW, NT
                        o = bank[3][0:NT, LSL * NS:(LSL + 1) * NS]
                    last = pe.transpose(o, sms[:, col:col + m], ident[0:NS, 0:NS])
                last.then_inc(sp_tr, 1)

            def sample_values(b):
                pe.wait_ge(spT_ready, 3 * (b + 1))
                pe.wait_ge(vc_in, 32 * (b + 1))
                for c in range(CT):
                    cols = slice(2 * c * NT, 2 * (c + 1) * NT)
                    o = bank[3][:, O_PV + 2 * c * NT:O_PV + 2 * (c + 1) * NT]
                    for s in range(FSL + LSL):
                        m = NFAR if s < FSL else P
                        pe.matmul(o, v_cache[0:m, s, c * P:(c + 1) * P], pTs[0:m, s, cols], start=(s == 0), stop=False)
                    last = pe.matmul(o, v_new[:, b, c * P:(c + 1) * P], pTs[0:NT, FSL + LSL, cols], start=False, stop=True)
                last.then_inc(spv_done, 1)

            keys_transposes(0)
            sample_scores(0)
            for b in range(NB):
                if b + 1 < NB:
                    keys_transposes(b + 1)
                sample_weights_T(b)
                if b + 1 < NB:
                    sample_scores(b + 1)
                sample_values(b)
            pe.wait_ge(cv, CK * CT * 2)
            pe.wait_ge(kc_evac, NB * CT * 3)
            pe.wait_ge(snm_done, NB)

            def conv_rows(n):
                if n >= 2:
                    pe.wait_ge(c_norm, n - 1)
                for c in range(CT):
                    last = pe.transpose(bank[n % 2][0:rows(n), c * P:(c + 1) * P], conv[:, c, n * P:n * P + rows(n)], ident[:, :])
                last.then_inc(c_tr, 1)

            conv_rows(0)
            for n in range(TILES):
                if n + 1 < TILES:
                    conv_rows(n + 1)
                pe.wait_ge(c_norm, n + 1)
                if n >= 2:
                    pe.wait_ge(c_T, CT * (n - 1))
                for c in range(CT):
                    last = pe.transpose(bank[2 + n % 2][:, c * P:c * P + rows(n)], cn[0:rows(n), n % 2, c * P:(c + 1) * P], ident[0:rows(n), 0:rows(n)])
                last.then_inc(c_tr2, 1)
            pe.wait_ge(c_T, CT * TILES)
            pe.wait_ge(satt_T, 2 * NB)
            pe.wait_ge(wout_in, 16)
            for n in range(TILES):
                if n >= 2:
                    pe.wait_ge(res_done, n - 1)
                for half in range(2):
                    for k in range(KD):
                        last = pe.matmul(bank[4 * (n % 2) + half][0:rows(n), :], mixedT[:, k, n * P:n * P + rows(n)], w_out[:, k, half * 512:(half + 1) * 512],
                                         start=(k == 0), stop=(k == KD - 1))
                last.then_inc(mix_done, 1)

            pe.wait_ge(peer_in, 16 * (5 + 2 * PH))
            pe.wait_ge(res_done, TILES)
            for g in range(4):
                for s in range(4):
                    last = pe.transpose(bank[g][:, s * NK:(s + 1) * NK], sk_in[:, 4 * g + s, :], iden2[:, :])
                last.then_inc(sk_tr, 1)
            pe.wait_ge(sk_T, 4)

            def x1_transpose():
                pe.wait_ge(a_x1, 16)
                for k in range(KD):
                    last = pe.transpose(bank[2 + k // 4][:, k % 4 * P:(k % 4 + 1) * P], x1n[:, k * P:(k + 1) * P], iden2[:, :])
                    if k % 4 == 3:
                        last.then_inc(a_xtr, 1)

            def route(h):
                if h == 0:
                    pe.wait_ge(a_xT, 2)
                if h >= 2:
                    pe.wait_ge(a_qc, h - 1)
                for side in range(2):
                    for k in range(KD):
                        last = pe.matmul(bank[4 + h % 2][:, side * P:(side + 1) * P], wq[:, k, (2 * h + side) * KEYC:(2 * h + side + 1) * KEYC],
                                         x1T[:, k, :], start=(k == 0), stop=(k == KD - 1))
                last.then_inc(a_q, 1)
                pe.wait_ge(a_qc, h + 1)
                if h >= 2:
                    pe.wait_ge(a_sc, h - 1)
                for side in range(2):
                    last = pe.matmul(bank[6 + h % 2][:, side * NK:(side + 1) * NK], qh[:, h % 2, side * P:(side + 1) * P], skT[:, 2 * h + side, :], start=True, stop=True)
                last.then_inc(a_s, 1)

            def tile(with_route, base_of):
                if with_route:
                    x1_transpose()
                for h in range(PH + 1):
                    if with_route and h < PH:
                        route(h)
                    if h:
                        for k in range((h - 1) * TOP, h * TOP):
                            pe.wait_ge(a_diag, k + 1)
                            pe.wait_ge(gv[k % V_RING], base_of(k))
                            for half in range(2):
                                last = pe.matmul(bank[half], diag[:, k % DG_RING, :], v_buf[:, k % V_RING, half * 512:(half + 1) * 512],
                                                 start=(k == 0), stop=(k == SLOTS - 1))
                            last.then_inc(a_pv, 1)

            def end_tile(last=a_pv, value=SLOTS):
                pe.wait_ge(last, value)
                pe.sem_inc(ended["pe"], 1)
                pe.wait_ge(go["pe"], 1)
                pe.sem_clear(go["pe"])

            x1_transpose()
            for h in range(PH):
                route(h)
            pe.wait_ge(a_sc, PH)
            end_tile(a_s, PH)
            with pe.Fori(0, PT) as n:
                tile(True, lambda k: n * (16 * SLOTS // V_RING) + 16 * (k // V_RING + 1))
                end_tile()
            tile(False, lambda k: PT * (16 * SLOTS // V_RING) + 16 * (k // V_RING + 1))


_INS = ["x_prompt", "x_sample", "cache_k_win", "cache_v_win", "state_conv", "w_in", "w_out", "conv_w", "conv_b", "conv_ln_g", "conv_ln_b",
        "ln1_g", "ln1_b", "w_query", "sub_keys", "expert_u", "expert_v", "ln2_g", "ln2_b"]
_OUTS = [(1, SEQ, D), (NB, NT, D), (1, 1, SEQ, H, E), (1, 1, SEQ, H, E), (1, 1, PAST, CC), (1, NB, WIN, H, E), (1, NB, WIN, H, E), (1, NB, PAST, CC)]


def kernel(**inputs):
    import concourse.bacc as bacc
    from concourse.bass_utils import run_bass_kernel_spmd as run

    nc = bacc.Bacc("TRN2", target_bir_lowering=False, num_devices=1)
    arrays = {n: np.ascontiguousarray(inputs[n]) for n in _INS}
    arrays.update(shape_constants())
    I = {n: nc.dram_tensor(f"in_{n}", a.shape, mybir.dt.from_np(a.dtype), kind="ExternalInput").ap() for n, a in arrays.items()}
    O = [nc.dram_tensor(f"out_{i}", s, F32, kind="ExternalOutput").ap() for i, s in enumerate(_OUTS)]
    build(nc, I, O)
    r = run(nc, [{f"in_{n}": a for n, a in arrays.items()}], core_ids=[0]).results[0]
    return tuple(r[f"out_{i}"] for i in range(len(_OUTS)))
```

```python
from contextlib import ExitStack

import numpy as np

import concourse.bass as bass
import concourse.mybir as mybir

F32 = mybir.dt.float32
U32 = mybir.dt.uint32
ALU = mybir.AluOpType
ACT = mybir.ActivationFunctionType
AX = mybir.AxisListType

P = 128
D = 1024
KD = D // P
SEQ = 1024
NB, NT = 8, 8
NS = NB * NT
TOK = SEQ + NS
PT = SEQ // P
TILES = PT + 1
H, E = 8, 64
AW = H * E
CC = D - AW
CT = CC // P
CK = 31
PAST = CK - 1
WIN = 2048
SCALE = E ** -0.5
BRANCHES = ((128, 1), (512, 4), (2048, 16))
MASKED = -1e30
LOWEST = -3.0e38
ALPHA = 2.0 ** 0.25
EPS = 1e-5
PH = 8
NK = 128
TOP = 16
SLOTS = PH * TOP
KEYC = 128

FAR = WIN - 512
NFAR = FAR // 16
FSL = NT
LSL = 4
KEYS = NT + FSL * NFAR + LSL * P
HALF = FSL // 2 * NFAR
C_NEW, C_FAR2, C_NEAR = HALF, HALF + NT, 2 * HALF + NT

ROWS_OUT = TILES + 2
SB = (4, 5, 6)
O_PV = 384
W_RING = 4
U_RING = 8
V_RING = 8
DG_RING = 4


def _count(d):
    return sum((d >= 0) & (d <= w) & (d % s == 0) for w, s in BRANCHES)


def _bias(d):
    n = _count(d)
    return np.where(n > 0, np.log(np.maximum(n, 1)) / SCALE, MASKED).astype(np.float32)


def shape_constants():
    q = np.arange(P)[:, None]
    prompt = _bias(q + (SEQ - P) - np.arange(SEQ)[None, :])
    pos = np.empty(KEYS, np.int64)
    far = np.arange(NFAR)
    for r in range(FSL):
        at = r * NFAR if r < 4 else C_FAR2 + (r - 4) * NFAR
        pos[at:at + NFAR] = 16 * far + r
    pos[C_NEW:C_NEW + NT] = WIN + np.arange(NT)
    for s in range(LSL):
        pos[C_NEAR + s * P:C_NEAR + (s + 1) * P] = FAR + LSL * np.arange(P) + s
    t = np.tile(np.arange(NT), H)[:, None]
    sample = _bias(WIN + t - pos[None, :])
    return {
        "c_ident": np.eye(P, dtype=np.float32),
        "c_prompt_bias": prompt,
        "c_sample_bias": sample,
        "c_stack": np.tile(np.eye(P, dtype=np.float32)[:NS], (2, 1)),
        "c_iota": np.tile(np.arange(TOP, dtype=np.float32), (P, 1)),
    }


def build(nc, I, O):
    y_p, y_s, nk_p, nv_p, nc_p, nk_s, nv_s, nc_s = O
    x1_d = nc.dram_tensor("x1_scratch", (TILES * P, D), F32, kind="Internal").ap()

    ctx = ExitStack()
    with ctx:
        base = nc.sbuf_base
        base = (base + 63) // 64 * 64
        names = [0]

        def at(off, shape, dt=F32):
            names[0] += 1
            return nc.alloc_sbuf_tensor_at(f"t{names[0]}", shape, dt, offset=base + off)

        def sem(name):
            return ctx.enter_context(nc.semaphore(name))

        psum = ctx.enter_context(nc.psum_tensor("psum", [P, 8 * 512], F32))
        bank = [psum[:, i * 512:(i + 1) * 512] for i in range(8)]

        o_a = 0
        o_b = o_a + KD * TOK * 4
        o_c = o_b + KD * D * 4
        o_d = o_c + 2 * CT * SEQ * 4 + PT * AW * 4
        cache_bytes = (FSL + LSL) * AW * 4
        o_f = o_c + 3 * cache_bytes
        assert o_f >= o_d + CT * (PAST + SEQ) * 4 + CT * NB * (PAST + NT) * 4
        o_g = o_f + CT * TOK * 4
        xT = at(o_a, [P, KD, TOK])
        mixedT = at(o_a, [P, KD, TOK])
        w_v = at(o_b, [P, KD, AW])
        w_ring = at(o_b + KD * AW * 4, [P, W_RING, KD, P])
        w_out = at(o_b, [P, KD, D])
        qT = at(o_c, [P, CT, SEQ])
        kT = at(o_c + CT * SEQ * 4, [P, CT, SEQ])
        v = at(o_c + 2 * CT * SEQ * 4, [P, PT, AW])
        k_cache = [at(o, [P, FSL + LSL, AW]) for o in (o_c, o_b)]
        v_cache = [at(o_c + n * cache_bytes, [P, FSL + LSL, AW]) for n in (1, 2)]
        gluP = at(o_d, [P, CT, PAST + SEQ])
        gluS = at(o_d + CT * (PAST + SEQ) * 4, [P, CT, NB, PAST + NT])
        conv = at(o_f, [P, CT, TOK])
        sm = at(o_g, [P, 2, SEQ])
        pT = at(o_g + 8192, [P, 2, SEQ])
        att = at(o_g + 16384, [P, 2, AW])
        o_h = o_g + 20480
        kTc = at(o_g, [P, CT, FSL * NFAR + LSL * P])
        xt = at(o_h, [P, 2, D])
        o_i = o_h + 8192
        bias_p = at(o_i, [P, SEQ])
        sig = at(o_i + 4096, [P, 2, 512])
        sms = at(o_i, [NS, KEYS])
        o_j = o_i + max(8192, KEYS * 4)
        bias_s = at(o_j, [NS, KEYS])
        o_k = o_j + KEYS * 4
        ident = at(o_k, [P, P])
        qTs = at(o_k + 512, [P, CT, NS])
        kTs = at(o_k + 1536, [P, CT, NS])
        glu_new = at(o_k + 2560, [P, CT, NS])
        cwT = at(o_k + 3584, [P, CT, CK + 3])
        o_l = o_k + 3584 + 576
        pTs = at(o_l, [P, FSL + LSL + 1, NS])
        small = at(o_l + 3328, [P, 64])
        o_m = o_l + 3328 + 256
        kst = at(o_m, [P, 2, AW])
        v_new = at(o_m, [NT, 2, AW])
        qbd = at(o_g + CT * 1280 * 4, [P, CT, NB, NS])
        assert CT * 1280 * 4 == 20480
        cw = at(o_f, [CK + 3, CC])
        st_in = at(o_f + 2048, [120, 2, CC])
        vs = at(o_f + 8192, [NS, AW])
        end_front = o_m + 4096
        assert base + end_front <= nc.sbuf_usable_end, (base + end_front, nc.sbuf_usable_end)
        lnw = at(o_g, [P, 2, D])
        xr = at(o_g + 8192, [P, 2, D])
        res = at(o_g + 16384, [P, 2, D])
        x1o = at(o_g + 24576, [P, 2, D])
        assert o_g + 32768 <= o_j
        stat = at(o_l, [P, 2, 32])
        cn = at(o_i, [P, 2, CC])
        cstat = at(o_l + 256, [P, 2, 16])
        stack = at(o_l + 512, [P, P])

        u_buf = at(0, [P, U_RING, D])
        v_buf = at(U_RING * D * 4, [P, V_RING, D])
        assert (U_RING + V_RING) * D * 4 <= o_c
        wq = at(o_c, [P, KD, PH * 2 * KEYC])

        class Region:

            def __init__(self, start, end):
                self.off, self.end = start, end

            def __call__(self, shape, dt=F32):
                n = (int(np.prod(shape[1:])) * 4 + 31) // 32 * 32
                self.off += n
                assert self.off <= self.end, shape
                return at(self.off - n, shape, dt)

        early = Region(o_c + KD * PH * 2 * KEYC * 4, o_g)
        skT = early([P, PH * 2, NK])
        x1T = early([P, KD, P])
        sk_in = at(early.off - KD * P * 4, [P, PH * 2, KEYC])
        x1n = early([P, D])
        qh = early([P, 2, 2 * P])
        sh = early([P, 2, 2 * NK])
        iota = early([P, TOP])
        tv = early([P, 2, TOP])
        ti = early([P, 2, TOP], U32)
        tif = early([P, 2, TOP])
        bv = early([P, TOP])
        bj = early([P, TOP], U32)
        ab = early([P, 2, TOP], U32)
        abf = early([P, 2, TOP])
        eif = early([P, 2, TOP])
        ex = early([P, 2, TOP])
        den = early([P, 4])
        rdn = early([P, 4])
        st2 = early([P, 32])
        idn = early([P, SLOTS], U32)
        gtn = early([P, SLOTS])
        scratch = Region(o_j, o_k)
        s2 = scratch([P, 2, NK])
        cand = scratch([P, TOP * TOP])
        cand2 = scratch([P, TOP * TOP])
        eq = scratch([P, 2, TOP * TOP])
        late = Region(o_g, o_i + 4096)
        x1c = late([P, D])
        junk = late([P, 2, D])
        lnw2 = late([P, 2, D])
        yt = late([P, D])
        res2 = late([P, D])
        diag = late([P, DG_RING, P])
        per_slot = Region(o_k + 512, o_k + 3584)
        idc = per_slot([P, SLOTS], U32)
        gtc = per_slot([P, SLOTS])
        dots = per_slot([P, SLOTS])
        gel = per_slot([P, SLOTS])
        coef = per_slot([P, SLOTS])

        const_in = sem("const_in")
        aux_in = sem("aux_in")
        x_in = [sem(f"x_in{i}") for i in range(2)]
        x_used = sem("x_used")
        xT_ready = sem("xT_ready")
        aux_tr = sem("aux_tr")
        aux_ready = sem("aux_ready")
        w_in_s = [sem(f"w_in{i}") for i in range(W_RING)]
        wv_in = sem("wv_in")
        proj_done = sem("proj_done")
        proj_evac = sem("proj_evac")
        glu_done = sem("glu_done")
        v_done = sem("v_done")
        v_evac = sem("v_evac")
        row_tr = sem("row_tr")
        row_evac = sem("row_evac")
        row_out = [sem(f"row_out{i}") for i in range(2)]
        out_dma = sem("out_dma")
        v_out = sem("v_out")
        vn_out = sem("vn_out")
        pads = sem("pads")
        glu_s = sem("glu_s")
        dv = sem("dv")
        cv = sem("cv")
        s_done = sem("s_done")
        nm_done = sem("nm_done")
        exp_done = sem("exp_done")
        p_tr = sem("p_tr")
        pT_ready = sem("pT_ready")
        pv_done = sem("pv_done")
        att_done = sem("att_done")
        att_tr = sem("att_tr")
        att_T = sem("att_T")
        kc_in = [sem(f"kc_in{i}") for i in range(2)]
        vc_in = [sem(f"vc_in{i}") for i in range(2)]
        qbd_done = sem("qbd_done")
        kc_tr = sem("kc_tr")
        kc_evac = sem("kc_evac")
        ss_done = sem("ss_done")
        snm_done = sem("snm_done")
        sexp_done = sem("sexp_done")
        sp_done = sem("sp_done")
        sp_tr = sem("sp_tr")
        spT_ready = sem("spT_ready")
        spv_done = sem("spv_done")
        satt_T = sem("satt_T")
        c_tr = sem("c_tr")
        c_var = sem("c_var")
        c_std = sem("c_std")
        c_norm = sem("c_norm")
        c_tr2 = sem("c_tr2")
        c_T = sem("c_T")
        wout_in = sem("wout_in")
        lnw_in = sem("lnw_in")
        xr_in = [sem(f"xr_in{i}") for i in range(2)]
        mix_done = sem("mix_done")
        res_done = sem("res_done")
        l_var = sem("l_var")
        l_std = sem("l_std")
        x1_done = sem("x1_done")
        x1_out = [sem(f"x1_out{i}") for i in range(2)]
        sk_loaded = sem("sk_loaded")
        wq_in = sem("wq_in")
        peer_in = sem("peer_in")
        y_stored = sem("y_stored")
        sk_tr = sem("sk_tr")
        sk_T = sem("sk_T")

        a_cur = sem("a_cur")
        a_x1 = sem("a_x1")
        a_xtr = sem("a_xtr")
        a_xT = sem("a_xT")
        a_q = sem("a_q")
        a_qc = sem("a_qc")
        a_s = sem("a_s")
        a_sc = sem("a_sc")
        a_route = sem("a_route")
        a_diff = sem("a_diff")
        a_exp = sem("a_exp")
        a_dot = sem("a_dot")
        a_gelu = sem("a_gelu")
        a_coef = sem("a_coef")
        a_diag = sem("a_diag")
        a_pv = sem("a_pv")
        a_var = sem("a_var")
        a_std = sem("a_std")
        a_y = sem("a_y")
        a_res = sem("a_res")
        a_up = sem("a_up")
        ch = sem("ch")
        tile_sems = [a_cur, a_x1, a_xtr, a_xT, a_q, a_qc, a_s, a_sc, a_route, a_diff, a_exp, a_dot,
                     a_gelu, a_coef, a_diag, a_pv, a_var, a_std, a_y, a_res, a_up, ch]
        ended = {e: sem(f"ended_{e}") for e in ("pe", "act", "dve", "pool")}
        go = {e: sem(f"go_{e}") for e in ("pe", "act", "dve", "pool")}
        gu = [sem(f"gu{i}") for i in range(U_RING)]
        gv = [sem(f"gv{i}") for i in range(V_RING)]

        def rows(n):
            return P if n < PT else NS

        xp, xs = I["x_prompt"][0], I["x_sample"].rearrange("b t d -> (b t) d")

        def x_rows(n):
            return xp[n * P:(n + 1) * P, :] if n < PT else xs

        w_cols = I["w_in"][0].rearrange("(k p) c -> p k c", p=P)
        CHUNKS = [("k", c) for c in range(CT)] + [("q", c) for c in range(CT)]
        for c in range(CT):
            CHUNKS += [("a", c), ("g", c)]
        COL = {"q": 0, "k": AW, "a": 3 * AW, "g": 3 * AW + CC}
        GROUPS = [(0, 512), (512, 512), (SEQ, NS)]
        NPROJ = len(CHUNKS) * len(GROUPS)
        UNITS = [(t, h) for t in range(PT) for h in range(H)]

        block = ctx.enter_context(nc.Block())

        @block.sync
        def _(sp):
            sp.dma_start(ident[:, :], I["c_ident"]).then_inc(const_in, 16)
            for n in range(2):
                sp.dma_start(xt[:, n, :], x_rows(n)).then_inc(x_in[n], 16)
            sp.dma_start(cw[0:CK, :], I["conv_w"][0]).then_inc(aux_in, 16)
            for i, name in enumerate(("conv_b", "conv_ln_g", "conv_ln_b")):
                sp.dma_start(cw[CK + i:CK + i + 1, :], I[name]).then_inc(aux_in, 16)
            sp.dma_start(st_in[:, :, :], I["state_conv"][0].rearrange("(g b) r c -> (b r) g c", g=2)).then_inc(aux_in, 16)
            for c in range(W_RING):
                kind, i = CHUNKS[c]
                sp.dma_start(w_ring[:, c, :, :], w_cols[:, :, COL[kind] + i * P:COL[kind] + (i + 1) * P]).then_inc(w_in_s[c], 16)
            for n in range(2, TILES):
                sp.wait_ge(x_used, n - 1)
                sp.dma_start(xt[0:rows(n), n % 2, :], x_rows(n)).then_inc(x_in[n % 2], 16)
            sp.dma_start(bias_p[:, :], I["c_prompt_bias"]).then_inc(const_in, 16)
            sp.dma_start(bias_s[:, :], I["c_sample_bias"]).then_inc(const_in, 16)
            sp.dma_start(w_v[:, :, :], w_cols[:, :, 2 * AW:3 * AW]).then_inc(wv_in, 16)
            for c in range(W_RING, len(CHUNKS)):
                kind, i = CHUNKS[c]
                sp.wait_ge(proj_done, 3 * (c - W_RING + 1))
                sp.dma_start(w_ring[:, c % W_RING, :, :], w_cols[:, :, COL[kind] + i * P:COL[kind] + (i + 1) * P]).then_inc(w_in_s[c % W_RING], 16)
            for n in range(PT):
                sp.wait_ge(v_evac, n + 1)
                sp.dma_start(nv_p[0, 0].rearrange("t h e -> t (h e)")[n * P:(n + 1) * P, :], v[:, n, :]).then_inc(v_out, 16)
            sp.wait_ge(v_evac, TILES)
            for b in range(NB):
                sp.dma_start(nv_s[0, b, WIN - NT:WIN].rearrange("t h e -> t (h e)"), vs[b * NT:(b + 1) * NT, :]).then_inc(vn_out, 16)
            for n in range(ROWS_OUT):
                sp.wait_ge(row_evac, n + 1)
                if n < PT:
                    sp.dma_start(nk_p[0, 0].rearrange("t h e -> t (h e)")[n * P:(n + 1) * P, :], kst[:, n % 2, :]).then_inc(row_out[n % 2], 16)
                elif n == PT:
                    for b in range(NB):
                        sp.dma_start(nk_s[0, b, WIN - NT:WIN].rearrange("t h e -> t (h e)"), kst[b * NT:(b + 1) * NT, n % 2, :]).then_inc(row_out[n % 2], 16)
                elif n == PT + 1:
                    sp.dma_start(nc_p[0, 0], kst[0:PAST, n % 2, :]).then_inc(row_out[n % 2], 16)
                else:
                    for b in range(NB):
                        sp.dma_start(nc_s[0, b, PAST - NT:PAST, :], kst[b * NT:(b + 1) * NT, n % 2, :]).then_inc(row_out[n % 2], 16)
            for b in range(NB):
                for new, old in ((nk_s, I["cache_k_win"]), (nv_s, I["cache_v_win"])):
                    sp.dma_start(new[0, b, 0:WIN - NT].rearrange("t h e -> (t h e)").rearrange("(a m) -> a m", a=256),
                                 old[0, b, NT:WIN].rearrange("t h e -> (t h e)").rearrange("(a m) -> a m", a=256)).then_inc(out_dma, 16)
            sp.dma_start(nc_s[0, :, 0:PAST - NT, :], I["state_conv"][0, :, NT:PAST, :]).then_inc(out_dma, 16)

            def load_cache(cache, b, dst, arrived):
                src = cache[0, b].rearrange("t h e -> t (h e)")
                sp.dma_start(dst[0:NFAR, 0:FSL, :], src[0:FAR, :].rearrange("(g r) c -> g r c", r=16)[:, 0:FSL, :]).then_inc(arrived, 16)
                sp.dma_start(dst[:, FSL:, :], src[FAR:WIN, :].rearrange("(p s) c -> p s c", s=LSL)).then_inc(arrived, 16)

            sp.wait_ge(proj_done, NPROJ)
            sp.wait_ge(v_done, TILES)
            load_cache(I["cache_k_win"], 1, k_cache[1], kc_in[1])
            sp.wait_ge(pv_done, len(UNITS))
            sp.wait_ge(v_out, 16 * PT)
            load_cache(I["cache_k_win"], 0, k_cache[0], kc_in[0])

            def load_values(b):
                load_cache(I["cache_v_win"], b, v_cache[b % 2], vc_in[b % 2])
                sp.dma_start(v_new[:, b % 2, :], nv_s[0, b, WIN - NT:WIN].rearrange("t h e -> t (h e)")).then_inc(vc_in[b % 2], 16)

            sp.wait_ge(vn_out, 16 * NB)
            sp.wait_ge(row_out[0], 16 * (PT // 2 + NB + NB))
            sp.wait_ge(row_out[1], 16 * (PT // 2 + 1))
            load_values(0)
            sp.wait_ge(cv, 2 * CK * CT)
            load_values(1)
            for b in range(1, NB):
                if b + 1 < NB:
                    sp.wait_ge(kc_tr, b * CT * 3)
                    load_cache(I["cache_k_win"], b + 1, k_cache[(b + 1) % 2], kc_in[(b + 1) % 2])
                    sp.wait_ge(spv_done, b)
                    load_values(b + 1)
            sp.wait_ge(kc_tr, NB * CT * 3)
            sp.dma_start(w_out[:, :, :], I["w_out"][0].rearrange("(k p) n -> p k n", p=P)).then_inc(wout_in, 16)
            sp.wait_ge(spv_done, NB)
            sp.dma_start(wq[:, :, :], I["w_query"][0].rearrange("(k p) n -> p k n", p=P)).then_inc(wq_in, 16)
            sp.dma_start(stack[:, :], I["c_stack"]).then_inc(peer_in, 16)
            for i, name in enumerate(("ln1_g", "ln1_b")):
                sp.dma_start(lnw[:, i, :], I[name].partition_broadcast(P)).then_inc(lnw_in, 16)
            for n in range(TILES):
                if n >= 2:
                    sp.wait_ge(res_done, n - 1)
                sp.dma_start(xr[0:rows(n), n % 2, :], x_rows(n)).then_inc(xr_in[n % 2], 16)
                if n == 0:
                    sp.wait_ge(c_tr, TILES)
                    for i in range(2 * PH):
                        sp.dma_start(sk_in[:, i, :], I["sub_keys"][0, i // 2, i % 2]).then_inc(sk_loaded, 16)
                    sp.dma_start(iota[:, :], I["c_iota"]).then_inc(sk_loaded, 16)
                if n:
                    sp.wait_ge(x1_done, n)
                    sp.dma_start(x1_d[(n - 1) * P:n * P, :], x1o[:, (n - 1) % 2, :]).then_inc(x1_out[(n - 1) % 2], 16)
                if n == 2:
                    sp.wait_ge(x1_out[0], 16)
                    sp.wait_ge(sk_tr, 4)
                    sp.dma_start(x1n[:, :], x1_d[0:P, :]).then_inc(a_x1, 16)
            sp.wait_ge(x1_done, TILES)
            sp.dma_start(x1_d[PT * P:PT * P + NS, :], x1o[0:NS, PT % 2, :]).then_inc(x1_out[PT % 2], 16)
            sp.dma_start(x1_d[PT * P + NS:TILES * P, :], x1o[0:NS, PT % 2, :]).then_inc(x1_out[PT % 2], 16)
            sp.wait_ge(x1_out[0], 16 * 6)
            sp.wait_ge(x1_out[1], 16 * 4)
            for i, name in enumerate(("ln2_g", "ln2_b")):
                sp.dma_start(lnw2[:, i, :], I[name].partition_broadcast(P)).then_inc(peer_in, 16)

            def between():
                for e in ended.values():
                    sp.wait_ge(e, 1)
                for s in [*tile_sems, *ended.values()]:
                    sp.sem_clear(s)
                for s in go.values():
                    sp.sem_inc(s, 1)

            def next_rows(n):
                sp.wait_ge(a_cur, 1)
                sp.dma_start(x1n[:, :], x1_d[bass.ds(n * P + P, P), :]).then_inc(a_x1, 16)

            between()
            next_rows(0)
            between()
            with sp.Fori(1, PT) as n:
                next_rows(n)
                sp.wait_ge(a_y, 1)
                sp.dma_start(y_p[0][bass.ds(n * P - P, P), :], yt[:, :]).then_inc(y_stored, 16)
                sp.wait_ge(y_stored, 16)
                sp.sem_clear(y_stored)
                between()
            sp.dma_start(idc[NS:P, 0:SLOTS // 2], idn[0:NS, SLOTS // 2:]).then_inc(a_up, 16)
            sp.dma_start(gtc[NS:P, 0:SLOTS // 2], gtn[0:NS, SLOTS // 2:]).then_inc(a_up, 16)
            sp.dma_start(x1c[NS:P, :], x1n[0:NS, :]).then_inc(a_up, 16)
            sp.wait_ge(a_y, 1)
            sp.dma_start(y_p[0][(PT - 1) * P:PT * P, :], yt[:, :]).then_inc(y_stored, 16)
            sp.wait_ge(y_stored, 16)
            sp.sem_inc(a_cur, 1)
            sp.wait_ge(a_y, 2)
            sp.dma_start(y_s.rearrange("b t d -> (b t) d"), yt[0:NS, :]).then_inc(y_stored, 16)
            sp.wait_ge(y_stored, 32)
            sp.wait_ge(out_dma, 16 * (2 * NB + 1))
            sp.wait_ge(v_out, 16 * PT)
            sp.wait_ge(row_out[0], 16 * (PT // 2 + NB + NB))
            sp.wait_ge(row_out[1], 16 * (PT // 2 + 1))

        @block.gpsimd
        def _(pool):
            def gathers(slots):
                for s in range(slots + TOP):
                    if s < slots:
                        if s >= U_RING:
                            pool.wait_ge(a_dot, s - U_RING + 1)
                        pool.indirect_dma_start(u_buf[:, s % U_RING, :], None, I["expert_u"][0],
                                                bass.IndirectOffsetOnAxis(ap=idc[:, s:s + 1], axis=0)).then_inc(gu[s % U_RING], 16)
                    r = s - TOP
                    if r >= 0:
                        if r >= V_RING:
                            pool.wait_ge(a_pv, r - V_RING + 1)
                        pool.indirect_dma_start(v_buf[:, r % V_RING, :], None, I["expert_v"][0],
                                                bass.IndirectOffsetOnAxis(ap=idc[:, r:r + 1], axis=0)).then_inc(gv[r % V_RING], 16)

            def end_tile():
                pool.sem_inc(ended["pool"], 1)
                pool.wait_ge(go["pool"], 1)
                pool.sem_clear(go["pool"])

            end_tile()
            pool.wait_ge(a_cur, 1)
            gathers(SLOTS)
            end_tile()
            with pool.Fori(1, PT) as n:
                pool.wait_ge(a_cur, 1)
                gathers(SLOTS)
                end_tile()
            pool.wait_ge(a_cur, 1)
            pool.wait_ge(a_up, 48)
            gathers(SLOTS // 2)

        @block.scalar
        def _(act):
            act.wait_ge(aux_tr, 1)
            act.activation(cwT[:, :, :], bank[4][:, 0:CT * (CK + 3)].rearrange("p (c k) -> p c k", c=CT), ACT.Copy).then_inc(aux_ready, 1)
            for g in range(2):
                act.wait_ge(aux_tr, 2 + g)
                act.activation(gluS[:, :, g * 4:g * 4 + 4, 0:PAST],
                               bank[5 + g][:, 0:CT * 120].rearrange("p (c b r) -> p c b r", c=CT, b=4), ACT.Copy).then_inc(aux_ready, 1)
            for n in range(TILES):
                act.wait_ge(x_used, n + 1)
                for half in range(2):
                    act.activation(xT[:, half * 4:half * 4 + 4, n * P:n * P + rows(n)],
                                   bank[2 * (n % 2) + half][:, :].rearrange("p (k t) -> p k t", k=4)[:, :, 0:rows(n)], ACT.Copy).then_inc(xT_ready, 1)
            ng = 0
            for c, (kind, i) in enumerate(CHUNKS):
                for g, (t0, tn) in enumerate(GROUPS):
                    j = 3 * c + g
                    act.wait_ge(proj_done, j + 1)
                    src = bank[4 + j % 4][:, 0:tn]
                    if kind in "qk":
                        full, new = (qT, qTs) if kind == "q" else (kT, kTs)
                        dst = full[:, i, t0:t0 + tn] if g < 2 else new[:, i, :]
                        act.activation(dst, src, ACT.Copy).then_inc(proj_evac, 1)
                    elif kind == "a":
                        dst = gluP[:, i, PAST + t0:PAST + t0 + tn] if g < 2 else glu_new[:, i, :]
                        act.activation(dst, src, ACT.Copy).then_inc(proj_evac, 1)
                    else:
                        if ng >= 2:
                            act.wait_ge(glu_done, ng - 1)
                        act.activation(sig[:, ng % 2, 0:tn], src, ACT.Sigmoid).then_inc(proj_evac, 1)
                        ng += 1
            for n in range(ROWS_OUT):
                act.wait_ge(row_tr, n + 1)
                if n in (2, 3, 4, 5, 6, 7, 8, 9, 10):
                    before = (n - 2) // 2 + 1
                    act.wait_ge(row_out[n % 2], 16 * (before if n < 10 else PT // 2 + NB))
                m = P if n < PT else NS if n in (PT, PT + 2) else PAST
                act.activation(kst[0:m, n % 2, :], bank[n % 4][0:m, :], ACT.Copy).then_inc(row_evac, 1)
            for i, (t, h) in enumerate(UNITS):
                L = (t + 1) * P
                act.wait_ge(nm_done, i + 1)
                act.activation(sm[:, i % 2, 0:L], sm[:, i % 2, 0:L], ACT.Exp, bias=small[:, 2 + i % 2:3 + i % 2], scale=SCALE,
                               accum_out=small[:, 4 + i % 2:5 + i % 2]).then_inc(exp_done, 1)
                act.wait_ge(p_tr, i + 1)
                if i >= 2:
                    act.wait_ge(pv_done, i - 1)
                act.activation(pT[:, i % 2, 0:L], psum[:, 4 * 512:4 * 512 + L], ACT.Copy).then_inc(pT_ready, 1)
                if (h == 0 and t) or i == len(UNITS) - 1:
                    d = t if i == len(UNITS) - 1 else t - 1
                    act.wait_ge(att_tr, d + 1)
                    act.activation(mixedT[:, 0:CT, d * P:(d + 1) * P], bank[7].rearrange("p (c q) -> p c q", c=CT), ACT.Copy).then_inc(att_T, 1)
            def keys_T(b):
                for c in range(CT):
                    for part in range(3):
                        act.wait_ge(kc_tr, (b * CT + c) * 3 + part + 1)
                        if b and c == 0 and part == 0:
                            act.wait_ge(ss_done, b)
                        w = HALF if part < 2 else LSL * P
                        act.activation(kTc[:, c, part * HALF:part * HALF + w], bank[part][:, 0:w], ACT.Copy).then_inc(kc_evac, 1)

            keys_T(0)
            for b in range(NB):
                act.wait_ge(snm_done, b + 1)
                act.activation(sms[:, :], sms[:, :], ACT.Exp, bias=small[0:NS, 8:9], scale=SCALE, accum_out=small[0:NS, 9:10]).then_inc(sexp_done, 1)
                if b + 1 < NB:
                    keys_T(b + 1)
                act.wait_ge(sp_tr, b + 1)
                if b:
                    act.wait_ge(spv_done, b)
                act.activation(pTs[0:NFAR, 0:FSL, :], bank[7][0:NFAR, :].rearrange("p (s q) -> p s q", s=FSL), ACT.Copy).then_inc(spT_ready, 1)
                act.activation(pTs[:, FSL:FSL + LSL, :], bank[3][:, 0:LSL * NS].rearrange("p (s q) -> p s q", s=LSL), ACT.Copy).then_inc(spT_ready, 1)
                act.activation(pTs[0:NT, FSL + LSL, :], bank[3][0:NT, LSL * NS:(LSL + 1) * NS], ACT.Copy).then_inc(spT_ready, 1)
                act.wait_ge(spv_done, b + 1)
                out = bank[3][:, O_PV:O_PV + CT * 2 * NT].rearrange("p (c u) -> p c u", c=CT)
                for u in range(2):
                    act.activation(mixedT[u * E:(u + 1) * E, 0:CT, SEQ + b * NT:SEQ + (b + 1) * NT],
                                   out[u * E:(u + 1) * E, :, u * NT:(u + 1) * NT], ACT.Copy).then_inc(satt_T, 1)
            for n in range(TILES):
                act.wait_ge(c_var, n + 1)
                act.activation(cstat[0:rows(n), n % 2, 9:10], cstat[0:rows(n), n % 2, 8:9], ACT.Sqrt).then_inc(c_std, 1)
                act.wait_ge(c_tr2, n + 1)
                for c in range(CT):
                    act.activation(mixedT[:, CT + c, n * P:n * P + rows(n)], bank[2 + n % 2][:, c * P:c * P + rows(n)], ACT.Silu,
                                   bias=cwT[:, c, CK + 2:CK + 3], scale=cwT[:, c, CK + 1:CK + 2]).then_inc(c_T, 1)
            def ln1_std(n):
                act.wait_ge(l_var, n + 1)
                act.activation(stat[0:rows(n), n % 2, 17:18], stat[0:rows(n), n % 2, 16:17], ACT.Sqrt).then_inc(l_std, 1)

            def x1_transposed(b0):
                for half in range(2):
                    act.wait_ge(a_xtr, half + 1)
                    act.activation(x1T[:, half * 4:half * 4 + 4, :], bank[b0 + half][:, :].rearrange("p (k t) -> p k t", k=4), ACT.Copy).then_inc(a_xT, 1)

            def route_copies(h):
                act.wait_ge(a_q, h + 1)
                act.activation(qh[:, h % 2, :], bank[4 + h % 2][:, 0:2 * P], ACT.Copy).then_inc(a_qc, 1)
                act.wait_ge(a_s, h + 1)
                if h >= 2:
                    act.wait_ge(a_route, h - 1)
                act.activation(sh[:, h % 2, :], bank[6 + h % 2][:, 0:2 * NK], ACT.Copy).then_inc(a_sc, 1)

            def gate_exp(h):
                act.wait_ge(a_diff, h + 1)
                act.activation(ex[:, h % 2, :], ex[:, h % 2, :], ACT.Exp, accum_out=den[:, h % 2:h % 2 + 1]).then_inc(a_exp, 1)

            def diags(h, eye):
                act.wait_ge(a_coef, h + 1)
                for k in range(h * TOP, (h + 1) * TOP):
                    if k >= DG_RING:
                        act.wait_ge(a_pv, k - DG_RING + 1)
                    act.activation(diag[:, k % DG_RING, :], eye[:, :], ACT.Copy, scale=coef[:, k:k + 1]).then_inc(a_diag, 1)

            def norm_std(m):
                act.wait_ge(a_var, m)
                act.activation(st2[:, 17:18], st2[:, 16:17], ACT.Sqrt).then_inc(a_std, 1)

            def tile(heads, route, norm, eye):
                if route:
                    x1_transposed(2)
                for h in range(heads + 1):
                    if route and h < PH:
                        route_copies(h)
                    if h:
                        diags(h - 1, eye)
                    if h < heads:
                        act.wait_ge(a_dot, (h + 1) * TOP)
                        act.activation(gel[:, h * TOP:(h + 1) * TOP], dots[:, h * TOP:(h + 1) * TOP], ACT.Gelu).then_inc(a_gelu, 1)
                        if h == 0 and norm:
                            norm_std(1)
                        if route:
                            gate_exp(h)

            def end_tile(last=a_diag, value=SLOTS):
                act.wait_ge(last, value)
                act.sem_inc(ended["act"], 1)
                act.wait_ge(go["act"], 1)
                act.sem_clear(go["act"])

            ln1_std(0)
            ln1_std(1)
            for g in range(4):
                act.wait_ge(sk_tr, g + 1)
                act.activation(skT[:, 4 * g:4 * g + 4, :], bank[4 + g].rearrange("p (s k) -> p s k", s=4), ACT.Copy).then_inc(sk_T, 1)
            ln1_std(2)
            x1_transposed(6)
            for h in range(PH):
                route_copies(h)
                gate_exp(h)
                if h + 3 < TILES:
                    ln1_std(h + 3)
            end_tile(a_exp, PH)
            tile(PH, True, False, ident)
            end_tile()
            with act.Fori(1, PT) as n:
                tile(PH, True, True, ident)
                end_tile()
            tile(PH // 2, False, True, stack)
            norm_std(2)

        @block.vector
        def _(dve):
            steps = [0]

            def seq(ins, s=dv):
                steps[0] += 1
                ins.then_inc(s, 1)
                dve.wait_ge(s, steps[0])

            for c in range(CT):
                dve.memset(gluP[:, c, 0:PAST], 0.0).then_inc(pads, 1)
            ng = 0
            for i in range(CT):
                for g, (t0, tn) in enumerate(GROUPS):
                    dve.wait_ge(proj_evac, 3 * (2 * CT + 2 * i + 1) + g + 1)
                    dst = gluP[:, i, PAST + t0:PAST + t0 + tn] if g < 2 else glu_new[:, i, :]
                    dve.tensor_tensor(dst, dst, sig[:, ng % 2, 0:tn], ALU.mult).then_inc(glu_done, 1)
                    ng += 1
            dve.wait_ge(glu_done, ng)
            dve.wait_ge(aux_ready, 3)
            for c in range(CT):
                dve.tensor_copy(gluS[:, c, :, PAST:], glu_new[:, c, :].rearrange("p (b t) -> p b t", b=NB)).then_inc(glu_s, 1)
            for n in range(TILES):
                dve.wait_ge(v_done, n + 1)
                dst = v[:, n, :] if n < PT else vs[:, :]
                dve.tensor_copy(dst, bank[4 + (NPROJ + n) % 4][0:rows(n), :]).then_inc(v_evac, 1)
            dve.wait_ge(pads, CT)
            dve.wait_ge(glu_s, CT)
            dve.wait_ge(vn_out, 16 * NB)
            taps = [(k, c, s) for k in range(CK) for c in range(CT) for s in range(2)]

            def tap(m):
                k, c, s = taps[m]
                if s == 0:
                    src, dst = gluP[:, c, k:k + SEQ], conv[:, c, 0:SEQ]
                else:
                    src, dst = gluS[:, c, :, k:k + NT], conv[:, c, SEQ:TOK].rearrange("p (b t) -> p b t", b=NB)
                w = cwT[:, c, k:k + 1]
                if k == 0:
                    dve.tensor_scalar(dst, src, w, cwT[:, c, CK:CK + 1], ALU.mult, ALU.add).then_inc(cv, 1)
                else:
                    dve.wait_ge(cv, m - 2 * CT + 1)
                    dve.scalar_tensor_tensor(dst, src, w, dst, ALU.mult, ALU.add).then_inc(cv, 1)

            def normalise(i):
                t, h = UNITS[i]
                dve.wait_ge(exp_done, i + 1)
                seq(dve.reciprocal(small[:, 6:7], small[:, 4 + i % 2:5 + i % 2]))
                dve.wait_ge(pv_done, i + 1)
                if h == 0 and t >= 2:
                    dve.wait_ge(att_tr, t - 1)
                dve.tensor_scalar(att[:, t % 2, h * E:(h + 1) * E], bank[6 + i % 2][:, 0:E], small[:, 6:7], None, ALU.mult).then_inc(att_done, 1)
                dve.wait_ge(att_done, i + 1)

            dve.wait_ge(const_in, 48)
            m = 0
            for i, (t, h) in enumerate(UNITS):
                L = (t + 1) * P
                dve.wait_ge(s_done, i + 1)
                if i >= 2:
                    dve.wait_ge(p_tr, i - 1)
                off = SEQ - L
                s0 = 2 * (i % 2) * 512
                seq(dve.tensor_tensor_reduce(out=sm[:, i % 2, 0:L], in0=psum[:, s0:s0 + L], in1=bias_p[:, off:SEQ], scale=1.0, scalar=LOWEST,
                                             op0=ALU.add, op1=ALU.max, accum_out=small[:, i % 2:i % 2 + 1]))
                dve.tensor_scalar(small[:, 2 + i % 2:3 + i % 2], small[:, i % 2:i % 2 + 1], -SCALE, None, ALU.mult).then_inc(nm_done, 1)
                for _ in range(4):
                    if m < len(taps):
                        tap(m)
                        m += 1
                if i:
                    normalise(i - 1)
            normalise(len(UNITS) - 1)
            while m < len(taps):
                tap(m)
                m += 1
            dve.wait_ge(pT_ready, len(UNITS))
            dve.wait_ge(x_used, TILES)
            seq(dve.memset(qbd[:, :, :, :], 0.0))
            for c in range(CT):
                for u in range(2):
                    hh = 2 * c + u
                    dve.tensor_copy(qbd[u * E:(u + 1) * E, c, :, hh * NT:(hh + 1) * NT],
                                    qTs[u * E:(u + 1) * E, c, :].rearrange("p (b t) -> p b t", b=NB)).then_inc(qbd_done, 1)
            for b in range(NB):
                dve.wait_ge(ss_done, b + 1)
                for lo, hi, bk in ((0, C_FAR2, 0), (C_FAR2, C_NEAR, 1), (C_NEAR, KEYS, 2)):
                    seq(dve.tensor_tensor(sms[:, lo:hi], bank[SB[bk]][0:NS, 0:hi - lo], bias_s[:, lo:hi], ALU.add))
                seq(dve.reduce_max(small[0:NS, 7:8], sms[:, :], AX.X))
                dve.tensor_scalar(small[0:NS, 8:9], small[0:NS, 7:8], -SCALE, None, ALU.mult).then_inc(snm_done, 1)
                dve.wait_ge(sexp_done, b + 1)
                seq(dve.reciprocal(small[0:NS, 10:11], small[0:NS, 9:10]))
                dve.tensor_scalar(sms[:, :], sms[:, :], small[0:NS, 10:11], None, ALU.mult).then_inc(sp_done, 1)
            for n in range(TILES):
                m_, s_ = rows(n), cstat[0:rows(n), n % 2, :]
                dve.wait_ge(c_tr, n + 1)
                seq(dve.bn_stats(s_[:, 0:6], bank[n % 2][0:m_, :]))
                seq(dve.bn_aggr(s_[:, 6:8], s_[:, 0:6]))
                dve.tensor_scalar(s_[:, 8:9], s_[:, 7:8], EPS, None, ALU.add).then_inc(c_var, 1)
                dve.wait_ge(c_std, n + 1)
                seq(dve.reciprocal(s_[:, 10:11], s_[:, 9:10]))
                if n >= 2:
                    dve.wait_ge(c_tr2, n - 1)
                dve.tensor_scalar(cn[0:m_, n % 2, :], bank[n % 2][0:m_, :], s_[:, 6:7], s_[:, 10:11], ALU.subtract, ALU.mult).then_inc(c_norm, 1)
            dve.wait_ge(lnw_in, 32)

            def ln1(n):
                m_, s_ = rows(n), stat[0:rows(n), n % 2, :]
                r_ = res[0:m_, n % 2, :]
                dve.wait_ge(mix_done, n + 1)
                dve.wait_ge(xr_in[n % 2], 16 * (n // 2 + 1))
                b0 = 2 * (n % 2)
                for half in range(2):
                    sl = slice(half * 512, half * 512 + 512)
                    seq(dve.scalar_tensor_tensor(r_[:, sl], xr[0:m_, n % 2, sl], ALPHA, bank[b0 + half][0:m_, :], ALU.mult, ALU.add))
                    seq(dve.bn_stats(s_[:, 6 * half:6 * half + 6], r_[:, sl]))
                dve.sem_inc(res_done, 1)
                seq(dve.bn_aggr(s_[:, 12:14], s_[:, 0:12]))
                dve.tensor_scalar(s_[:, 16:17], s_[:, 13:14], EPS, None, ALU.add).then_inc(l_var, 1)
                dve.wait_ge(l_std, n + 1)
                seq(dve.reciprocal(s_[:, 18:19], s_[:, 17:18]))
                seq(dve.tensor_scalar(r_, r_, s_[:, 12:13], s_[:, 18:19], ALU.subtract, ALU.mult))
                seq(dve.tensor_tensor(r_, r_, lnw[0:m_, 0, :], ALU.mult))
                if n >= 2:
                    dve.wait_ge(x1_out[n % 2], 16 * (n // 2))
                dve.tensor_tensor(x1o[0:m_, n % 2, :], r_, lnw[0:m_, 1, :], ALU.add).then_inc(x1_done, 1)

            local = [0]

            def step(ins):
                local[0] += 1
                ins.then_inc(ch, 1)
                dve.wait_ge(ch, local[0])

            def best(vals, idx, scores, spare):
                step(dve.max(vals[:, 0:8], scores))
                step(dve.match_replace(spare, vals[:, 0:8], scores, LOWEST))
                step(dve.max(vals[:, 8:16], spare))
                step(dve.max_index(idx[:, 0:8], vals[:, 0:8], scores))
                step(dve.max_index(idx[:, 8:16], vals[:, 8:16], spare))

            def route(h):
                dve.wait_ge(a_sc, h + 1)
                for side in range(2):
                    best(tv[:, side, :], ti[:, side, :], sh[:, h % 2, side * NK:(side + 1) * NK], s2[:, side, :])
                step(dve.tensor_copy(tif[:, :, :], ti[:, :, :]))
                step(dve.tensor_tensor(cand[:, :].rearrange("p (a b) -> p a b", a=TOP),
                                       tv[:, 0, :].unsqueeze(2).broadcast_to([P, TOP, TOP]),
                                       tv[:, 1, :].unsqueeze(1).broadcast_to([P, TOP, TOP]), ALU.add))
                best(bv[:, :], bj[:, :], cand[:, :], cand2[:, :])
                step(dve.tensor_scalar(ex[:, h % 2, :], bv[:, :], bv[:, 0:1], None, ALU.subtract))
                dve.sem_inc(a_diff, 1)
                step(dve.tensor_scalar(ab[:, 0, :], bj[:, :], 4, None, ALU.logical_shift_right))
                step(dve.tensor_scalar(ab[:, 1, :], bj[:, :], 15, None, ALU.bitwise_and))
                step(dve.tensor_copy(abf[:, :, :], ab[:, :, :]))
                for side in range(2):
                    e3 = eq[:, side, :].rearrange("p (k r) -> p k r", k=TOP)
                    step(dve.tensor_tensor(e3, abf[:, side, :].unsqueeze(2).broadcast_to([P, TOP, TOP]),
                                           iota[:, :].unsqueeze(1).broadcast_to([P, TOP, TOP]), ALU.is_equal))
                    step(dve.tensor_tensor(e3, e3, tif[:, side, :].unsqueeze(1).broadcast_to([P, TOP, TOP]), ALU.mult))
                    step(dve.reduce_sum(eif[:, side, :], e3, AX.X))
                step(dve.scalar_tensor_tensor(idn[:, h * TOP:(h + 1) * TOP], eif[:, 0, :], float(NK), eif[:, 1, :], ALU.mult, ALU.add))
                dve.wait_ge(a_exp, h + 1)
                step(dve.reciprocal(rdn[:, h % 2:h % 2 + 1], den[:, h % 2:h % 2 + 1]))
                step(dve.tensor_scalar(gtn[:, h * TOP:(h + 1) * TOP], ex[:, h % 2, :], rdn[:, h % 2:h % 2 + 1], None, ALU.mult))
                dve.sem_inc(a_route, 1)

            def residual():
                for half in range(2):
                    sl = slice(half * 512, half * 512 + 512)
                    dve.scalar_tensor_tensor(res2[:, sl], x1c[:, sl], ALPHA, bank[half], ALU.mult, ALU.add).then_inc(a_res, 1)

            def norm(m, m_=P):
                r_, s_ = res2[0:m_, :], st2[0:m_, :]
                for half in range(2):
                    sl = slice(half * 512, half * 512 + 512)
                    step(dve.bn_stats(s_[:, 6 * half:6 * half + 6], r_[:, sl]))
                step(dve.bn_aggr(s_[:, 12:14], s_[:, 0:12]))
                dve.tensor_scalar(s_[:, 16:17], s_[:, 13:14], EPS, None, ALU.add).then_inc(a_var, 1)
                dve.wait_ge(a_std, m)
                step(dve.reciprocal(s_[:, 18:19], s_[:, 17:18]))
                step(dve.tensor_scalar(r_, r_, s_[:, 12:13], s_[:, 18:19], ALU.subtract, ALU.mult))
                step(dve.tensor_tensor(r_, r_, lnw2[0:m_, 0, :], ALU.mult))
                dve.tensor_tensor(yt[0:m_, :], r_, lnw2[0:m_, 1, :], ALU.add).then_inc(a_y, 1)

            def tile(heads, with_route, with_norm, base_of, m_=P):
                step(dve.tensor_copy(idc[0:m_, 0:heads * TOP], idn[0:m_, 0:heads * TOP]))
                step(dve.tensor_copy(x1c[0:m_, :], x1n[0:m_, :]))
                step(dve.tensor_copy(gtc[0:m_, 0:heads * TOP], gtn[0:m_, 0:heads * TOP]))
                dve.sem_inc(a_cur, 1)
                if heads < PH:
                    dve.wait_ge(a_up, 48)
                for h in range(heads):
                    for k in range(h * TOP, (h + 1) * TOP):
                        if k >= 2:
                            dve.wait_ge(a_dot, k - 1)
                        dve.wait_ge(gu[k % U_RING], base_of(k))
                        dve.tensor_tensor_reduce(out=junk[:, k % 2, :], in0=u_buf[:, k % U_RING, :], in1=x1c[:, :], scale=1.0,
                                                 scalar=0.0, op0=ALU.mult, op1=ALU.add, accum_out=dots[:, k:k + 1]).then_inc(a_dot, 1)
                    dve.wait_ge(a_gelu, h + 1)
                    hs = slice(h * TOP, (h + 1) * TOP)
                    dve.tensor_tensor(coef[:, hs], gel[:, hs], gtc[:, hs], ALU.mult).then_inc(a_coef, 1)
                    if h == 0 and with_norm:
                        norm(1)
                    if with_route:
                        route(h)
                dve.wait_ge(a_dot, heads * TOP)
                dve.wait_ge(a_pv, heads * TOP)
                residual()

            def end_tile(last=a_res, value=2):
                dve.wait_ge(last, value)
                dve.sem_inc(ended["dve"], 1)
                dve.wait_ge(go["dve"], 1)
                dve.sem_clear(go["dve"])
                local[0] = 0

            for n in range(3):
                ln1(n)
            dve.wait_ge(sk_loaded, 16 * (2 * PH + 1))
            for h in range(PH):
                route(h)
                if h + 3 < TILES:
                    ln1(h + 3)
            dve.wait_ge(x1_done, TILES)
            dve.wait_ge(x1_out[0], 16 * 6)
            dve.wait_ge(x1_out[1], 16 * 4)
            end_tile(a_route, PH)
            dve.wait_ge(peer_in, 16 * 3)
            rounds = 16 * SLOTS // U_RING
            tile(PH, True, False, lambda k: 16 * (k // U_RING + 1))
            end_tile()
            with dve.Fori(1, PT) as n:
                tile(PH, True, True, lambda k: n * rounds + 16 * (k // U_RING + 1))
                end_tile()
            tile(PH // 2, False, True, lambda k: PT * rounds + 16 * (k // U_RING + 1), NS)
            dve.wait_ge(a_res, 2)
            dve.wait_ge(a_cur, 2)
            norm(2)

        @block.tensor
        def _(pe):
            pe.wait_ge(const_in, 16)
            pe.wait_ge(aux_in, 16 * 5)
            for c in range(CT):
                last = pe.transpose(bank[4][:, c * (CK + 3):(c + 1) * (CK + 3)], cw[0:CK + 3, c * P:(c + 1) * P], ident[0:CK + 3, 0:CK + 3])
            last.then_inc(aux_tr, 1)
            for g in range(2):
                for c in range(CT):
                    last = pe.transpose(bank[5 + g][:, c * 120:(c + 1) * 120], st_in[0:120, g, c * P:(c + 1) * P], ident[0:120, 0:120])
                last.then_inc(aux_tr, 1)
            for n in range(TILES):
                pe.wait_ge(x_in[n % 2], 16 * (n // 2 + 1))
                if n >= 2:
                    pe.wait_ge(xT_ready, 2 * (n - 1))
                for k in range(KD):
                    last = pe.transpose(bank[2 * (n % 2) + k // 4][:, k % 4 * P:k % 4 * P + rows(n)], xt[0:rows(n), n % 2, k * P:(k + 1) * P],
                                        ident[0:rows(n), 0:rows(n)])
                last.then_inc(x_used, 1)
            pe.wait_ge(xT_ready, 2 * TILES)
            pe.wait_ge(aux_ready, 3)
            for c in range(len(CHUNKS)):
                pe.wait_ge(w_in_s[c % W_RING], 16 * (c // W_RING + 1))
                for g, (t0, tn) in enumerate(GROUPS):
                    j = 3 * c + g
                    if j >= 4:
                        pe.wait_ge(proj_evac, j - 3)
                    for k in range(KD):
                        last = pe.matmul(bank[4 + j % 4][:, 0:tn], w_ring[:, c % W_RING, k, :], xT[:, k, t0:t0 + tn], start=(k == 0), stop=(k == KD - 1))
                    last.then_inc(proj_done, 1)
            pe.wait_ge(wv_in, 16)
            for n in range(TILES):
                if n < 4:
                    pe.wait_ge(proj_evac, NPROJ - 3 + n)
                else:
                    pe.wait_ge(v_evac, n - 3)
                for k in range(KD):
                    last = pe.matmul(bank[4 + (NPROJ + n) % 4][0:rows(n), :], xT[:, k, n * P:n * P + rows(n)], w_v[:, k, :], start=(k == 0), stop=(k == KD - 1))
                last.then_inc(v_done, 1)
            pe.wait_ge(glu_done, 3 * CT)
            for n in range(ROWS_OUT):
                if n >= 4:
                    pe.wait_ge(row_evac, n - 3)
                for c in range(CT):
                    if n < PT:
                        src, m = kT[:, c, n * P:(n + 1) * P], P
                    elif n == PT:
                        src, m = kTs[:, c, :], NS
                    elif n == PT + 1:
                        src, m = gluP[:, c, SEQ:SEQ + PAST], PAST
                    else:
                        src, m = glu_new[:, c, :], NS
                    last = pe.transpose(bank[n % 4][0:m, c * P:(c + 1) * P], src, ident[:, :])
                last.then_inc(row_tr, 1)
            pe.wait_ge(row_evac, ROWS_OUT)
            pe.wait_ge(v_evac, TILES)

            def scores(i):
                t, h = UNITS[i]
                c, r = h // 2, E * (h % 2)
                L = (t + 1) * P
                if i >= 2:
                    pe.wait_ge(nm_done, i - 1)
                for half in range(0, (L + 511) // 512):
                    w = min(512, L - half * 512)
                    last = pe.matmul(bank[2 * (i % 2) + half][:, 0:w], qT[r:r + E, c, t * P:(t + 1) * P], kT[r:r + E, c, half * 512:half * 512 + w],
                                     start=True, stop=True)
                last.then_inc(s_done, 1)

            def weights_T(i):
                t, h = UNITS[i]
                pe.wait_ge(exp_done, i + 1)
                if i:
                    pe.wait_ge(pT_ready, i)
                for j in range(t + 1):
                    last = pe.transpose(bank[4 + j // 4][:, j % 4 * P:(j % 4 + 1) * P], sm[:, i % 2, j * P:(j + 1) * P], ident[:, :])
                last.then_inc(p_tr, 1)

            def values(i):
                t, h = UNITS[i]
                pe.wait_ge(pT_ready, i + 1)
                if i >= 2:
                    pe.wait_ge(att_done, i - 1)
                if h == 1 and t:
                    pe.wait_ge(att_T, t)
                for j in range(t + 1):
                    last = pe.matmul(bank[6 + i % 2][:, 0:E], pT[:, i % 2, j * P:(j + 1) * P], v[:, j, h * E:(h + 1) * E], start=(j == 0), stop=(j == t))
                last.then_inc(pv_done, 1)

            def att_transposes(t):
                pe.wait_ge(att_done, (t + 1) * H)
                for c in range(CT):
                    last = pe.transpose(bank[7][:, c * P:(c + 1) * P], att[:, t % 2, c * P:(c + 1) * P], ident[:, :])
                last.then_inc(att_tr, 1)

            scores(0)
            for i in range(len(UNITS)):
                if i + 1 < len(UNITS):
                    scores(i + 1)
                if i:
                    values(i - 1)
                weights_T(i)
                if i and i % H == 0:
                    att_transposes(i // H - 1)
            values(len(UNITS) - 1)
            att_transposes(PT - 1)
            pe.wait_ge(att_T, PT)
            pe.wait_ge(qbd_done, 2 * CT)
            def keys_transposes(b):
                pe.wait_ge(kc_in[b % 2], 32 * (b // 2 + 1))
                for c in range(CT):
                    for part in range(3):
                        if b or c:
                            pe.wait_ge(kc_evac, (b * CT + c - 1) * 3 + part + 1)
                        for s in range(4):
                            if part < 2:
                                last = pe.transpose(bank[part][:, s * NFAR:(s + 1) * NFAR], k_cache[b % 2][0:NFAR, part * 4 + s, c * P:(c + 1) * P], ident[0:NFAR, 0:NFAR])
                            else:
                                last = pe.transpose(bank[part][:, s * P:(s + 1) * P], k_cache[b % 2][:, FSL + s, c * P:(c + 1) * P], ident[:, :])
                        last.then_inc(kc_tr, 1)

            def sample_scores(b):
                pe.wait_ge(kc_evac, (b + 1) * CT * 3)
                if b:
                    pe.wait_ge(snm_done, b)
                for part in range(3):
                    o = bank[SB[part]]
                    w = HALF if part < 2 else LSL * P
                    for c in range(CT):
                        last = pe.matmul(o[0:NS, 0:w], qbd[:, c, b, :], kTc[:, c, part * HALF:part * HALF + w], start=(c == 0), stop=(c == CT - 1))
                    if part == 0:
                        for c in range(CT):
                            last = pe.matmul(o[0:NS, HALF:HALF + NT], qbd[:, c, b, :], kTs[:, c, b * NT:(b + 1) * NT], start=(c == 0), stop=(c == CT - 1))
                last.then_inc(ss_done, 1)

            def sample_weights_T(b):
                pe.wait_ge(sp_done, b + 1)
                if b:
                    pe.wait_ge(spT_ready, 3 * b)
                    pe.wait_ge(satt_T, 2 * b)
                for s in range(FSL + LSL + 1):
                    if s < FSL:
                        col, m = (s * NFAR if s < 4 else C_FAR2 + (s - 4) * NFAR), NFAR
                        o = bank[7][0:NFAR, s * NS:(s + 1) * NS]
                    elif s < FSL + LSL:
                        col, m = C_NEAR + (s - FSL) * P, P
                        o = bank[3][:, (s - FSL) * NS:(s - FSL + 1) * NS]
                    else:
                        col, m = C_NEW, NT
                        o = bank[3][0:NT, LSL * NS:(LSL + 1) * NS]
                    last = pe.transpose(o, sms[:, col:col + m], ident[0:NS, 0:NS])
                last.then_inc(sp_tr, 1)

            def sample_values(b):
                pe.wait_ge(spT_ready, 3 * (b + 1))
                pe.wait_ge(vc_in[b % 2], 48 * (b // 2 + 1))
                for c in range(CT):
                    cols = slice(2 * c * NT, 2 * (c + 1) * NT)
                    o = bank[3][:, O_PV + 2 * c * NT:O_PV + 2 * (c + 1) * NT]
                    for s in range(FSL + LSL):
                        m = NFAR if s < FSL else P
                        pe.matmul(o, v_cache[b % 2][0:m, s, c * P:(c + 1) * P], pTs[0:m, s, cols], start=(s == 0), stop=False)
                    last = pe.matmul(o, v_new[:, b % 2, c * P:(c + 1) * P], pTs[0:NT, FSL + LSL, cols], start=False, stop=True)
                last.then_inc(spv_done, 1)

            keys_transposes(0)
            sample_scores(0)
            for b in range(NB):
                if b + 1 < NB:
                    keys_transposes(b + 1)
                sample_weights_T(b)
                if b + 1 < NB:
                    sample_scores(b + 1)
                sample_values(b)
            pe.wait_ge(cv, CK * CT * 2)
            pe.wait_ge(kc_evac, NB * CT * 3)
            pe.wait_ge(snm_done, NB)

            def conv_rows(n):
                if n >= 2:
                    pe.wait_ge(c_norm, n - 1)
                for c in range(CT):
                    last = pe.transpose(bank[n % 2][0:rows(n), c * P:(c + 1) * P], conv[:, c, n * P:n * P + rows(n)], ident[:, :])
                last.then_inc(c_tr, 1)

            conv_rows(0)
            for n in range(TILES):
                if n + 1 < TILES:
                    conv_rows(n + 1)
                pe.wait_ge(c_norm, n + 1)
                if n >= 2:
                    pe.wait_ge(c_T, CT * (n - 1))
                for c in range(CT):
                    last = pe.transpose(bank[2 + n % 2][:, c * P:c * P + rows(n)], cn[0:rows(n), n % 2, c * P:(c + 1) * P], ident[0:rows(n), 0:rows(n)])
                last.then_inc(c_tr2, 1)
            pe.wait_ge(c_T, CT * TILES)
            pe.wait_ge(satt_T, 2 * NB)
            pe.wait_ge(wout_in, 16)
            def out_projection(n):
                if n >= 2:
                    pe.wait_ge(res_done, n - 1)
                for half in range(2):
                    for k in range(KD):
                        last = pe.matmul(bank[2 * (n % 2) + half][0:rows(n), :], mixedT[:, k, n * P:n * P + rows(n)], w_out[:, k, half * 512:(half + 1) * 512],
                                         start=(k == 0), stop=(k == KD - 1))
                last.then_inc(mix_done, 1)

            def x1_transpose(b0):
                pe.wait_ge(a_x1, 16)
                for k in range(KD):
                    last = pe.transpose(bank[b0 + k // 4][:, k % 4 * P:(k % 4 + 1) * P], x1n[:, k * P:(k + 1) * P], ident[:, :])
                    if k % 4 == 3:
                        last.then_inc(a_xtr, 1)

            def route(h):
                if h == 0:
                    pe.wait_ge(a_xT, 2)
                if h >= 2:
                    pe.wait_ge(a_qc, h - 1)
                for side in range(2):
                    for k in range(KD):
                        last = pe.matmul(bank[4 + h % 2][:, side * P:(side + 1) * P], wq[:, k, (2 * h + side) * KEYC:(2 * h + side + 1) * KEYC],
                                         x1T[:, k, :], start=(k == 0), stop=(k == KD - 1))
                last.then_inc(a_q, 1)
                pe.wait_ge(a_qc, h + 1)
                if h >= 2:
                    pe.wait_ge(a_sc, h - 1)
                for side in range(2):
                    last = pe.matmul(bank[6 + h % 2][:, side * NK:(side + 1) * NK], qh[:, h % 2, side * P:(side + 1) * P], skT[:, 2 * h + side, :], start=True, stop=True)
                last.then_inc(a_s, 1)

            def tile(heads, with_route, base_of):
                if with_route:
                    x1_transpose(2)
                for h in range(heads + 1):
                    if with_route and h < PH:
                        route(h)
                    if h:
                        for k in range((h - 1) * TOP, h * TOP):
                            pe.wait_ge(a_diag, k + 1)
                            pe.wait_ge(gv[k % V_RING], base_of(k))
                            for half in range(2):
                                last = pe.matmul(bank[half], diag[:, k % DG_RING, :], v_buf[:, k % V_RING, half * 512:(half + 1) * 512],
                                                 start=(k == 0), stop=(k == heads * TOP - 1))
                            last.then_inc(a_pv, 1)

            def end_tile(last=a_pv, value=SLOTS):
                pe.wait_ge(last, value)
                pe.sem_inc(ended["pe"], 1)
                pe.wait_ge(go["pe"], 1)
                pe.sem_clear(go["pe"])

            for n in range(3):
                out_projection(n)
            pe.wait_ge(sk_loaded, 16 * (2 * PH + 1))
            for g in range(4):
                for s in range(4):
                    last = pe.transpose(bank[4 + g][:, s * NK:(s + 1) * NK], sk_in[:, 4 * g + s, :], ident[:, :])
                last.then_inc(sk_tr, 1)
            pe.wait_ge(sk_T, 4)
            x1_transpose(6)
            pe.wait_ge(wq_in, 16)
            for h in range(PH):
                route(h)
                if h + 3 < TILES:
                    out_projection(h + 3)
            end_tile(a_s, PH)
            rounds = 16 * SLOTS // V_RING
            tile(PH, True, lambda k: 16 * (k // V_RING + 1))
            end_tile()
            with pe.Fori(1, PT) as n:
                tile(PH, True, lambda k: n * rounds + 16 * (k // V_RING + 1))
                end_tile()
            tile(PH // 2, False, lambda k: PT * rounds + 16 * (k // V_RING + 1))


_INS = ["x_prompt", "x_sample", "cache_k_win", "cache_v_win", "state_conv", "w_in", "w_out", "conv_w", "conv_b", "conv_ln_g", "conv_ln_b",
        "ln1_g", "ln1_b", "w_query", "sub_keys", "expert_u", "expert_v", "ln2_g", "ln2_b"]
_OUTS = [(1, SEQ, D), (NB, NT, D), (1, 1, SEQ, H, E), (1, 1, SEQ, H, E), (1, 1, PAST, CC), (1, NB, WIN, H, E), (1, NB, WIN, H, E), (1, NB, PAST, CC)]


def kernel(**inputs):
    import concourse.bacc as bacc
    from concourse.bass_utils import run_bass_kernel_spmd as run

    nc = bacc.Bacc("TRN2", target_bir_lowering=False, num_devices=1)
    arrays = {n: np.ascontiguousarray(inputs[n]) for n in _INS}
    arrays.update(shape_constants())
    I = {n: nc.dram_tensor(f"in_{n}", a.shape, mybir.dt.from_np(a.dtype), kind="ExternalInput").ap() for n, a in arrays.items()}
    O = [nc.dram_tensor(f"out_{i}", s, F32, kind="ExternalOutput").ap() for i, s in enumerate(_OUTS)]
    build(nc, I, O)
    r = run(nc, [{f"in_{n}": a for n, a in arrays.items()}], core_ids=[0]).results[0]
    return tuple(r[f"out_{i}"] for i in range(len(_OUTS)))
```
